# Optimizing a Trainium2 kernel written in Bass

```python
import jax, jax.numpy as jnp
from jax import lax
import numpy as np

D_MODEL = 1024
BATCH = 1
SEQ = 128
DEPTH = 2
DEC_BATCH = 1
DEC_SEQ = 512
PAST_LEN = 128

GRID_W = 64
HEAD_DIM = 64
N_BRANCH = 4
BRANCH_W = D_MODEL // 4
HGRN_HEADS = BRANCH_W // HEAD_DIM
HGRN_DK = HEAD_DIM
HGRN_DV = HEAD_DIM
HGRN_CHUNK = 64
NA_HEADS = BRANCH_W // HEAD_DIM
NA_ROWS = 8
NA_COLS = 16
SMLP_GROUPS = 4
SMLP_CHUNK = 128
SWA_HEADS = BRANCH_W // HEAD_DIM
SWA_KV_HEADS = SWA_HEADS // 2
SWA_WINDOW = 128
SWA_BLOCK = 128
ROPE_THETA = 10000.0
N_GROUPS = 4
EXPERTS_PER_GROUP = 4
N_EXPERTS = N_GROUPS * EXPERTS_PER_GROUP
EXPERT_FF = 256
TOP_K_INNER = 2
ADA_CHUNKS = 6
EPS = 1e-6
TINY = 1e-30
IN_SPLIT_SIZES = (BRANCH_W, BRANCH_W, BRANCH_W, BRANCH_W, BRANCH_W,
                  BRANCH_W, BRANCH_W, BRANCH_W,
                  BRANCH_W, BRANCH_W,
                  SWA_HEADS * HEAD_DIM, SWA_KV_HEADS * HEAD_DIM, SWA_KV_HEADS * HEAD_DIM,
                  N_BRANCH * D_MODEL)
P_IN = sum(IN_SPLIT_SIZES)

kernel_name = "hybrid_diffusion_ctx_prefix_step"

def rmsnorm(x, g=None):
    x32 = x.astype(jnp.float32)
    y = x32 * lax.rsqrt(jnp.mean(x32 * x32, axis=-1, keepdims=True) + EPS)
    if g is not None:
        y = y * g.astype(jnp.float32)
    return y.astype(x.dtype)

def adaln(cond, w, b):
    m = jax.nn.silu(cond) @ w + b
    return jnp.split(m[:, None, :], ADA_CHUNKS, axis=-1)

def split_cols(z):
    offs = [int(o) for o in np.cumsum(IN_SPLIT_SIZES)[:-1]]
    return jnp.split(z, offs, axis=-1)

def rope_2d(x):
    T, hd = x.shape[1], x.shape[-1]
    half = hd // 2
    t = jnp.arange(T)
    rows = (t // GRID_W).astype(jnp.float32)
    cols = (t % GRID_W).astype(jnp.float32)
    inv = 1.0 / (ROPE_THETA ** (jnp.arange(0, half, 2, dtype=jnp.float32) / half))

    def rot(xa, pos):
        ang = pos[:, None] * inv[None, :]
        cos = jnp.cos(ang)[None, :, None, :]
        sin = jnp.sin(ang)[None, :, None, :]
        x1, x2 = jnp.split(xa, 2, axis=-1)
        return jnp.concatenate([x1 * cos - x2 * sin, x1 * sin + x2 * cos], axis=-1)

    x32 = x.astype(jnp.float32)
    return jnp.concatenate([rot(x32[..., :half], rows), rot(x32[..., half:], cols)], axis=-1).astype(x.dtype)

def hgrn_scan(q, k, v, logf, s0):
    B, L, H, _ = q.shape
    n = L // HGRN_CHUNK

    def to_chunks(a):
        return jnp.moveaxis(a.reshape(B, n, HGRN_CHUNK, *a.shape[2:]), 1, 0)

    tri = jnp.tril(jnp.ones((HGRN_CHUNK, HGRN_CHUNK), dtype=bool))

    def step(S, inp):
        qc, kc, vc, lc = inp
        b = jnp.cumsum(lc, axis=1)
        inter = jnp.einsum('bthd,bhde->bthe', qc * jnp.exp(b), S)
        diff = b[:, :, None] - b[:, None, :]
        decay = jnp.exp(jnp.where(tri[None, :, :, None, None], diff, -jnp.inf))
        scores = jnp.einsum('btshd,bshd->bhts', qc[:, :, None] * decay, kc)
        intra = jnp.einsum('bhts,bshe->bthe', scores, vc)
        bl = b[:, -1]
        S = jnp.exp(bl)[..., None] * S + jnp.einsum('bshd,bshe->bhde', kc * jnp.exp(bl[:, None] - b), vc)
        return S, inter + intra

    S, o = lax.scan(step, s0, (to_chunks(q), to_chunks(k), to_chunks(v), to_chunks(logf)))
    o = jnp.moveaxis(o, 0, 1).reshape(B, L, H, v.shape[-1])
    return o, S

def hgrn_mixer(hq, hi, hff, hfb, hog, lb, onorm_g, s0):
    B, L, _ = hq.shape
    heads = lambda a: a.astype(jnp.float32).reshape(B, L, HGRN_HEADS, -1)
    flip = lambda a: a[:, ::-1]
    q = jax.nn.silu(heads(hq))
    v = heads(hi)
    lb32 = lb.astype(jnp.float32).reshape(2, HGRN_HEADS, HGRN_DK)

    def forget(z, lbd):
        f = lbd + (1.0 - lbd) * jax.nn.sigmoid(z)
        return jnp.log(jnp.maximum(f, TINY)), 1.0 - f

    lf_f, k_f = forget(heads(hff), lb32[0])
    lf_b, k_b = forget(heads(hfb), lb32[1])
    s0 = s0.astype(jnp.float32)
    o_f, s_f = hgrn_scan(q, k_f, v, lf_f, s0[:, 0])
    o_b, s_b = hgrn_scan(flip(q), flip(k_b), flip(v), flip(lf_b), s0[:, 1])
    o = o_f + flip(o_b)
    o = o * lax.rsqrt(jnp.mean(o * o, axis=-1, keepdims=True) + EPS) * onorm_g.astype(jnp.float32).reshape(HGRN_HEADS, HGRN_DV)
    out = o.reshape(B, L, -1) * jax.nn.silu(hog.astype(jnp.float32))
    return out.astype(hq.dtype), jnp.stack([s_f, s_b], axis=1)

def ctx_attention(q, k, v, sink):
    B, L = q.shape[:2]
    s = jnp.einsum('bqhgd,bkhd->bhgqk', q, k).astype(jnp.float32) * (HEAD_DIM ** -0.5)
    if sink is not None:
        s_sink = jnp.broadcast_to(sink.astype(jnp.float32)[None, :, :, None, None], s.shape[:-1] + (1,))
        s = jnp.concatenate([s, s_sink], axis=-1)
    p = jax.nn.softmax(s, axis=-1)
    if sink is not None:
        p = p[..., :-1]
    out = jnp.einsum('bhgqk,bkhd->bqhgd', p.astype(v.dtype), v)
    return out.reshape(B, L, -1)

def na_latent(q, k, v, kc, vc, rpb):
    B, T = q.shape[:2]
    R = T // GRID_W
    WR = min(NA_ROWS, R)
    grid = lambda a: a.reshape(B, R, GRID_W, NA_HEADS, HEAD_DIM)
    q, k, v = grid(q), grid(k), grid(v)
    r = jnp.arange(R)
    row_start = jnp.clip(r - WR // 2, 0, R - WR)
    row_idx = row_start[:, None] + jnp.arange(WR)[None, :]
    kg = k[:, row_idx]
    vg = v[:, row_idx]
    col = jnp.arange(GRID_W)
    col_start = jnp.clip(col - NA_COLS // 2, 0, GRID_W - NA_COLS)
    col_mask = (col[None, :] >= col_start[:, None]) & (col[None, :] < col_start[:, None] + NA_COLS)
    d_row = row_idx - r[:, None] + (NA_ROWS - 1)
    d_col = jnp.clip(col[None, :] - col[:, None], -(NA_COLS - 1), NA_COLS - 1) + (NA_COLS - 1)
    bias = rpb[:, d_row[:, None, :, None], d_col[None, :, None, :]]
    scale = HEAD_DIM ** -0.5
    s_lat = jnp.einsum('brqhd,brikhd->bhrqik', q, kg).astype(jnp.float32) * scale + bias.astype(jnp.float32)
    s_lat = jnp.where(col_mask[:, None, :], s_lat, -jnp.inf)
    s_ctx = jnp.einsum('brqhd,bchd->bhrqc', q, kc).astype(jnp.float32) * scale
    n_lat = WR * GRID_W
    p = jax.nn.softmax(jnp.concatenate([s_lat.reshape(B, NA_HEADS, R, GRID_W, n_lat), s_ctx], axis=-1), axis=-1).astype(v.dtype)
    p_lat = p[..., :n_lat].reshape(s_lat.shape)
    p_ctx = p[..., n_lat:]
    out = jnp.einsum('bhrqik,brikhd->brqhd', p_lat, vg) + jnp.einsum('bhrqc,bchd->brqhd', p_ctx, vc)
    return out.reshape(B, T, -1)

def chunk_mlp(mu, mv, ws, b):
    B, L, _ = mu.shape
    n = L // SMLP_CHUNK
    v = rmsnorm(mv.reshape(B, n, SMLP_CHUNK, SMLP_GROUPS, -1))
    mixed = jnp.einsum('gts,bnsgc->bntgc', ws, v) + b.T[None, None, :, :, None]
    return (mu.reshape(B, n, SMLP_CHUNK, SMLP_GROUPS, -1) * mixed).reshape(B, L, -1)

def swa_latent(q, k, v, kc, vc, sink):
    B, T = q.shape[:2]
    nb = T // SWA_BLOCK
    G = SWA_HEADS // SWA_KV_HEADS
    qb = q.reshape(B, nb, SWA_BLOCK, SWA_KV_HEADS, G, HEAD_DIM)

    def band(a):
        ab = a.reshape(B, nb, SWA_BLOCK, SWA_KV_HEADS, HEAD_DIM)
        ap = jnp.pad(ab, ((0, 0), (1, 1), (0, 0), (0, 0), (0, 0)))
        return jnp.concatenate([ap[:, :-2], ap[:, 1:-1], ap[:, 2:]], axis=2)

    kb, vb = band(k), band(v)
    qpos = jnp.arange(nb)[:, None] * SWA_BLOCK + jnp.arange(SWA_BLOCK)[None, :]
    kpos = (jnp.arange(nb)[:, None] - 1) * SWA_BLOCK + jnp.arange(3 * SWA_BLOCK)[None, :]
    rel = kpos[:, None, :] - qpos[:, :, None]
    mask = (jnp.abs(rel) <= SWA_WINDOW) & (kpos[:, None, :] >= 0) & (kpos[:, None, :] < T)
    scale = HEAD_DIM ** -0.5
    s_band = jnp.einsum('bnqhgd,bnjhd->bhgnqj', qb, kb).astype(jnp.float32) * scale
    s_band = jnp.where(mask, s_band, -jnp.inf)
    s_ctx = jnp.einsum('bnqhgd,bchd->bhgnqc', qb, kc).astype(jnp.float32) * scale
    s_sink = jnp.broadcast_to(sink.astype(jnp.float32).reshape(SWA_KV_HEADS, G)[None, :, :, None, None, None], s_band.shape[:-1] + (1,))
    p = jax.nn.softmax(jnp.concatenate([s_band, s_ctx, s_sink], axis=-1), axis=-1).astype(v.dtype)
    nj = 3 * SWA_BLOCK
    C = kc.shape[1]
    out = jnp.einsum('bhgnqj,bnjhd->bnqhgd', p[..., :nj], vb) + jnp.einsum('bhgnqc,bchd->bnqhgd', p[..., nj:nj + C], vc)
    return out.reshape(B, T, -1)

def merge_branches(branches, gates, w_branch, w_out):
    br = jnp.stack(branches, axis=2)
    proj = jnp.einsum('blnc,ncd->blnd', br, w_branch)
    g = jax.nn.sigmoid(gates.reshape(*gates.shape[:2], N_BRANCH, D_MODEL))
    return jnp.sum(g * proj, axis=2) @ w_out

def hier_moe(h, w_rg, b_rg, w_re, b_re, w_gate, w_up, w_down):
    g_logits = (h @ w_rg + b_rg).astype(jnp.float32)
    g_prob = jax.nn.softmax(g_logits, axis=-1)
    g_top_p, g_idx = lax.top_k(g_prob, 1)
    e_logits = (h @ w_re + b_re).astype(jnp.float32).reshape(*h.shape[:-1], N_GROUPS, EXPERTS_PER_GROUP)
    e_sel = jnp.sum(jax.nn.one_hot(g_idx[..., 0], N_GROUPS, dtype=jnp.float32)[..., None] * e_logits, axis=-2)
    e_top, e_idx = lax.top_k(e_sel, TOP_K_INNER)
    w = jax.nn.softmax(e_top, axis=-1) * g_top_p
    expert = g_idx * EXPERTS_PER_GROUP + e_idx
    combine = jnp.sum(jax.nn.one_hot(expert, N_EXPERTS, dtype=jnp.float32) * w[..., None], axis=-2).astype(h.dtype)
    a = jax.nn.silu(jnp.einsum('...d,edf->...ef', h, w_gate)) * jnp.einsum('...d,edf->...ef', h, w_up)
    return jnp.einsum('...ef,efd->...d', a * combine[..., None], w_down)

def pre_mix(x, cond, lw):
    sh1, sc1, g1, sh2, sc2, g2 = adaln(cond, lw['w_ada'], lw['b_ada'])
    h = rmsnorm(x, lw['norm1_g']) * (1 + sc1) + sh1
    return split_cols(h @ lw['w_in']), (g1, sh2, sc2, g2)

def post_mix(x, branches, gates, mods, lw):
    g1, sh2, sc2, g2 = mods
    x = x + g1 * merge_branches(branches, gates, lw['w_branch'], lw['w_out'])
    h = rmsnorm(x, lw['norm2_g']) * (1 + sc2) + sh2
    return x + g2 * hier_moe(h, lw['router_g_w'], lw['router_g_b'], lw['router_e_w'], lw['router_e_b'],
                             lw['moe_w_gate'], lw['moe_w_up'], lw['moe_w_down'])

def context_layer(x, c_ctx, lw):
    parts, mods = pre_mix(x, c_ctx[None, :], lw)
    hq, hi, hff, hfb, hog, naq, nak, nav, mu, mv, sq, sk, sv, gates = parts
    B, L = x.shape[:2]
    heads = lambda a, n: a.reshape(B, L, n, HEAD_DIM)
    s_zero = jnp.zeros((B, 2, HGRN_HEADS, HGRN_DK, HGRN_DV), jnp.float32)
    a_out, s_hgrn = hgrn_mixer(hq, hi, hff, hfb, hog, lw['lb'], lw['hgrn_onorm_g'], s_zero)
    na_k, na_v = heads(nak, NA_HEADS), heads(nav, NA_HEADS)
    b_out = ctx_attention(naq.reshape(B, L, NA_HEADS, 1, HEAD_DIM), na_k, na_v, None)
    c_out = chunk_mlp(mu, mv, lw['smlp_ws'], lw['smlp_b'])
    G = SWA_HEADS // SWA_KV_HEADS
    swa_k, swa_v = heads(sk, SWA_KV_HEADS), heads(sv, SWA_KV_HEADS)
    d_out = ctx_attention(sq.reshape(B, L, SWA_KV_HEADS, G, HEAD_DIM), swa_k, swa_v, lw['swa_sink'].reshape(SWA_KV_HEADS, G))
    x = post_mix(x, (a_out, b_out, c_out, d_out), gates, mods, lw)
    return x, na_k, na_v, swa_k, swa_v, s_hgrn.astype(x.dtype)

def latent_layer(x, c, lw, ck_na, cv_na, ck_swa, cv_swa, s_hgrn):
    parts, mods = pre_mix(x, c, lw)
    hq, hi, hff, hfb, hog, naq, nak, nav, mu, mv, sq, sk, sv, gates = parts
    B, T = x.shape[:2]
    heads = lambda a, n: a.reshape(B, T, n, HEAD_DIM)
    a_out, _ = hgrn_mixer(hq, hi, hff, hfb, hog, lw['lb'], lw['hgrn_onorm_g'], s_hgrn)
    b_out = na_latent(heads(naq, NA_HEADS), heads(nak, NA_HEADS), heads(nav, NA_HEADS), ck_na, cv_na, lw['na_rpb'])
    c_out = chunk_mlp(mu, mv, lw['smlp_ws'], lw['smlp_b'])
    d_out = swa_latent(rope_2d(heads(sq, SWA_HEADS)), rope_2d(heads(sk, SWA_KV_HEADS)), heads(sv, SWA_KV_HEADS),
                       ck_swa, cv_swa, lw['swa_sink'])
    return post_mix(x, (a_out, b_out, c_out, d_out), gates, mods, lw)

def setup_inputs(seed: int = 0) -> dict:
    key = jax.random.key(seed)
    ks = jax.random.split(key, 40)
    nrm = lambda k, shape, s: jax.random.normal(k, shape, jnp.float32) * s
    return {
        "x_prompt": nrm(ks[0], (BATCH, SEQ, D_MODEL), 1.0),
        "x_sample": nrm(ks[1], (DEC_BATCH, DEC_SEQ, D_MODEL), 1.0),
        "c": nrm(ks[2], (DEC_BATCH, D_MODEL), 1.0),
        "cache_na_k": nrm(ks[3], (DEC_BATCH, DEPTH, PAST_LEN, NA_HEADS, HEAD_DIM), 1.0),
        "cache_na_v": nrm(ks[4], (DEC_BATCH, DEPTH, PAST_LEN, NA_HEADS, HEAD_DIM), 1.0),
        "cache_swa_k": nrm(ks[5], (DEC_BATCH, DEPTH, PAST_LEN, SWA_KV_HEADS, HEAD_DIM), 1.0),
        "cache_swa_v": nrm(ks[6], (DEC_BATCH, DEPTH, PAST_LEN, SWA_KV_HEADS, HEAD_DIM), 1.0),
        "state_hgrn": nrm(ks[7], (DEC_BATCH, DEPTH, 2, HGRN_HEADS, HGRN_DK, HGRN_DV), 0.5),
        "c_ctx": nrm(ks[8], (D_MODEL,), 1.0),
        "w_ada": nrm(ks[9], (DEPTH, D_MODEL, ADA_CHUNKS * D_MODEL), 0.5 * D_MODEL ** -0.5),
        "b_ada": nrm(ks[10], (DEPTH, ADA_CHUNKS * D_MODEL), 0.02),
        "norm1_g": 1.0 + nrm(ks[11], (DEPTH, D_MODEL), 0.02),
        "norm2_g": 1.0 + nrm(ks[12], (DEPTH, D_MODEL), 0.02),
        "w_in": nrm(ks[13], (DEPTH, D_MODEL, P_IN), D_MODEL ** -0.5),
        "hgrn_lb": nrm(ks[14], (DEPTH, 2, BRANCH_W), 1.0),
        "hgrn_onorm_g": 1.0 + nrm(ks[15], (DEPTH, BRANCH_W), 0.02),
        "na_rpb": nrm(ks[16], (DEPTH, NA_HEADS, 2 * NA_ROWS - 1, 2 * NA_COLS - 1), 0.1),
        "smlp_ws": nrm(ks[17], (DEPTH, SMLP_GROUPS, SMLP_CHUNK, SMLP_CHUNK), SMLP_CHUNK ** -0.5),
        "smlp_b": 1.0 + nrm(ks[18], (DEPTH, SMLP_GROUPS, SMLP_CHUNK), 0.02),
        "swa_sink": nrm(ks[19], (DEPTH, SWA_HEADS), 0.5),
        "w_branch": nrm(ks[20], (DEPTH, N_BRANCH, BRANCH_W, D_MODEL), BRANCH_W ** -0.5),
        "w_out": nrm(ks[21], (DEPTH, D_MODEL, D_MODEL), D_MODEL ** -0.5),
        "router_g_w": nrm(ks[22], (DEPTH, D_MODEL, N_GROUPS), D_MODEL ** -0.5),
        "router_g_b": nrm(ks[23], (DEPTH, N_GROUPS), 0.01),
        "router_e_w": nrm(ks[24], (DEPTH, D_MODEL, N_EXPERTS), D_MODEL ** -0.5),
        "router_e_b": nrm(ks[25], (DEPTH, N_EXPERTS), 0.01),
        "moe_w_gate": nrm(ks[26], (DEPTH, N_EXPERTS, D_MODEL, EXPERT_FF), D_MODEL ** -0.5),
        "moe_w_up": nrm(ks[27], (DEPTH, N_EXPERTS, D_MODEL, EXPERT_FF), D_MODEL ** -0.5),
        "moe_w_down": nrm(ks[28], (DEPTH, N_EXPERTS, EXPERT_FF, D_MODEL), EXPERT_FF ** -0.5),
        "final_g": 1.0 + nrm(ks[29], (D_MODEL,), 0.02),
    }

def reference(x_prompt, x_sample, c, cache_na_k, cache_na_v, cache_swa_k, cache_swa_v, state_hgrn,
              c_ctx, w_ada, b_ada, norm1_g, norm2_g, w_in, hgrn_lb, hgrn_onorm_g, na_rpb, smlp_ws, smlp_b,
              swa_sink, w_branch, w_out, router_g_w, router_g_b, router_e_w, router_e_b,
              moe_w_gate, moe_w_up, moe_w_down, final_g):
    lb_soft = jax.nn.softmax(hgrn_lb.astype(jnp.float32), axis=0)
    lb_all = jnp.cumsum(lb_soft, axis=0) - lb_soft[0:1]
    lws = [dict(w_ada=w_ada[l], b_ada=b_ada[l], norm1_g=norm1_g[l], norm2_g=norm2_g[l], w_in=w_in[l],
                lb=lb_all[l], hgrn_onorm_g=hgrn_onorm_g[l], na_rpb=na_rpb[l], smlp_ws=smlp_ws[l],
                smlp_b=smlp_b[l], swa_sink=swa_sink[l], w_branch=w_branch[l], w_out=w_out[l],
                router_g_w=router_g_w[l], router_g_b=router_g_b[l], router_e_w=router_e_w[l],
                router_e_b=router_e_b[l], moe_w_gate=moe_w_gate[l], moe_w_up=moe_w_up[l],
                moe_w_down=moe_w_down[l]) for l in range(DEPTH)]

    xp = x_prompt
    na_ks, na_vs, swa_ks, swa_vs, hgrn_ss = [], [], [], [], []
    for l in range(DEPTH):
        xp, nk, nv, sk, sv, ss = context_layer(xp, c_ctx, lws[l])
        na_ks.append(nk); na_vs.append(nv); swa_ks.append(sk); swa_vs.append(sv); hgrn_ss.append(ss)
    y_prompt = rmsnorm(xp, final_g)
    new_na_k = jnp.stack(na_ks, axis=1)
    new_na_v = jnp.stack(na_vs, axis=1)
    new_swa_k = jnp.stack(swa_ks, axis=1)
    new_swa_v = jnp.stack(swa_vs, axis=1)
    new_hgrn_state = jnp.stack(hgrn_ss, axis=1)

    xs = x_sample
    for l in range(DEPTH):
        xs = latent_layer(xs, c, lws[l], cache_na_k[:, l], cache_na_v[:, l], cache_swa_k[:, l],
                          cache_swa_v[:, l], state_hgrn[:, l])
    y_sample = rmsnorm(xs, final_g)
    return (y_prompt, y_sample, new_na_k, new_na_v, new_swa_k, new_swa_v, new_hgrn_state)


_drawn_inputs = setup_inputs


def setup_inputs(seed=0):
    import zlib

    import numpy as np

    out = dict(_drawn_inputs(seed))
    spreads = {}
    factors = {'cache_na_k': 3.035,
     'cache_na_v': 2.683,
     'cache_swa_k': 4.265,
     'cache_swa_v': 3.573,
     'state_hgrn': 8.0,
     'norm1_g': 2.788,
     'norm2_g': 3.313,
     'hgrn_onorm_g': 8.0,
     'na_rpb': 8.0,
     'smlp_b': 6.458,
     'swa_sink': 64.0,
     'router_g_b': 6.569,
     'router_e_b': 7.547,
     'final_g': 8.388}
    for name, (base, spread) in spreads.items():
        noise = np.random.default_rng([zlib.crc32(name.encode()), seed]).standard_normal(out[name].shape)
        drawn = base * np.exp(spread * noise) if base else spread * noise
        out[name] = __import__('jax').numpy.asarray(drawn.astype(out[name].dtype))
    for name, factor in factors.items():
        out[name] = (out[name] * factor).astype(out[name].dtype)
    return out
```

```python
from contextlib import ExitStack

import numpy as np

import concourse.bass as bass
from concourse import mybir

F32 = mybir.dt.float32
U8 = mybir.dt.uint8
ALU = mybir.AluOpType
ACT = mybir.ActivationFunctionType
AX = mybir.AxisListType

P = 128
D = 1024
DEPTH = 2
CTX = 128
LAT = 512
T = LAT + CTX
KT = D // P
TILES = T // P
LT = LAT // P
CT = LT
BW = 256
HD = 64
HEADS = BW // HD
NB = 4
GROUPS = 4
EPG = 4
FF = 256
EPS = 1e-6
LN_SPLIT = 2.0 ** 50
TINY = 1e-30
FILL_LEVELS = [(0, 1, 2, 3), (4, 5, 6), (7,)]
FILLS = len(FILL_LEVELS)
LEVELS = 7
NEG = -1e30

UNIT = KT * P
RING = 4

HQ, HOG, NAQ, NAK, MU, SQ, SK = 0, 2, 4, 6, 8, 10, 12
N_FM = 13
BRANCH_AT = [HQ, NAQ, MU, SQ]

COL = dict(hq=0, hi=256, hff=512, hfb=768, hog=1024, naq=1280, nak=1536, nav=1792, mu=2048, mv=2304,
           sq=2560, sk=2816, sv=2944, gates=3072)

HGRN_UNITS = [(0, 0, CT)] + [(0, 1, i) for i in range(LT)] + [(1, 0, CT)] + [(1, 1, i) for i in reversed(range(LT))]
ATT_UNITS = [(b, h, i) for b in ("na", "swa") for h in range(HEADS) for i in range(TILES)]


class Job:
    def __init__(self, kind, arg, units=()):
        self.kind, self.arg, self.units = kind, arg, tuple(units)


def make_plan():
    units, parts = [], {}

    def take(*specs):
        at = len(units)
        units.extend(specs)
        return list(range(at, at + len(specs)))

    def ada(i):
        return [Job("ada", i, take(("ada", 2 * i), ("ada", 2 * i + 1)))]

    def fm(name, dst):
        u = take(("in", COL[name]), ("in", COL[name] + P))
        return [Job("fm", (name, dst + a, 0), [u[a]]) for a in range(2)]

    def tm(name):
        u = take(("tm", COL[name], 0), ("tm", COL[name], 1))
        return [Job("tm", (name, 0, LT, 256), u), Job("tm", (name, LT, TILES, 256), u)]

    parts["ada"] = sum([ada(i) for i in range(8)], [])
    parts["hgrn_in"] = (tm("hff") + ada(8) + tm("hfb") + ada(9) + tm("hi") + ada(10) + fm("hq", HQ) + ada(11)
                        + fm("hog", HOG) + ada(12))
    parts["hgrn_out"] = [Job("onorm", a) for a in range(2)]
    mix = fm("nak", NAK) + ada(13) + fm("naq", NAQ) + ada(14) + tm("nav") + ada(15) + tm("mv") + ada(16)
    u = take(("in", COL["sk"]), ("in", COL["sv"]))
    mix += [Job("fm", ("sk", SK, 0), [u[0]]), Job("tm", ("sv", 0, LT, P), [u[1]]), Job("tm", ("sv", LT, TILES, P), [u[1]])]
    mix += ada(17) + fm("sq", SQ) + ada(18) + fm("mu", MU) + ada(19)
    mix += [Job("rope", t) for t in (SK, SQ, SQ + 1)] + [Job("mlp", a) for a in range(2)]
    parts["mix_in"] = mix
    merge = []
    for dp in range(KT // 2):
        for d in (2 * dp, 2 * dp + 1):
            u = take(("branch", d), *[("in", COL["gates"] + n * D + d * P) for n in range(NB)])
            for n in range(NB):
                merge += [Job("gate", (d, n), [u[1 + n]]), Job("proj", (d, n), [u[0]])]
        merge += ada(20 + dp)
    parts["merge"] = merge
    out = []
    for d in range(0, KT, 2):
        u = take(("out", d), ("out", d + 1))
        out += [Job("out", d + a, [u[a]]) for a in range(2)]
    parts["out"] = out
    before = len(units)
    moe = [Job("cb", e) for e in range(EPG)]
    for e in range(EPG):
        for ft in range(2):
            u = take(("moe_gate", e, ft), ("moe_up", e, ft))
            moe += [Job("mgate", (e, ft), [u[0]]), Job("mup", (e, ft), [u[1]])]
    for d in range(0, KT, 2):
        u = take(("moe_down", d), ("moe_down", d + 1))
        moe += [Job("down", d + a, [u[a]]) for a in range(2)]
    group_units = units[before:]
    parts["moe"] = moe
    jobs = [j for p in parts.values() for j in p]
    read_by = {}
    for n, j in enumerate(jobs):
        for x in j.units:
            read_by[x // 2] = n + 1
    start, n = {}, 0
    for name, p in parts.items():
        start[name] = n
        n += len(p)
    return units[:before], group_units, parts, start, read_by


UNITS0, UNITS_G, PARTS, START, READ_BY = make_plan()
PAIRS0 = len(UNITS0) // 2
PAIRS_G = len(UNITS_G) // 2
PAIRS = PAIRS0 + GROUPS * PAIRS_G
JOBS_G = len(PARTS["moe"])
JOBS = START["moe"] + GROUPS * JOBS_G
assert START["moe"] % 2 == 0 and JOBS_G % 2 == 0 and PAIRS0 % RING == 0 and PAIRS_G % RING == 0


def read_by(pair):
    return READ_BY[pair]


def job_at(part, kind, arg):
    for n, j in enumerate(PARTS[part]):
        if j.kind == kind and (j.arg == arg or (kind in ("fm", "tm") and j.arg[:2] == arg)):
            return START[part] + n
    raise KeyError((part, kind, arg))


LPA, n = {}, 0
for name, w in (("nab", HEADS * 14 * HD), ("nk", 2 * P), ("nv", BW), ("sk", P), ("sv", P), ("ws", 4 * P),
                ("smb", 2 * P), ("sink", HEADS)):
    LPA[name] = (n, n + w)
    n += w
N_LPA = n
LPB, n = {}, 0
for name, w in (("b_ada", 48), ("n1", KT), ("n2", KT), ("on", 2), ("wr", KT * 20), ("rb", 20)):
    LPB[name] = (n, n + w)
    n += w
N_LPB = n
CST, n = {}, 0
for name, w in (("ident", P), ("ones", P), ("block", P), ("perm", P), ("decay", 2 * 8 * P), ("tail", 2 * P),
                ("cos", LAT), ("sin", LAT), ("swm", 3 * P), ("nam", HD)):
    CST[name] = (n, n + w)
    n += w
N_CST = n


def key_range(b, i):
    if i == CT:
        return LAT, T
    if b == "na":
        return 0, LAT
    return max(0, i - 1) * P, min(LT, i + 2) * P


def n_keys(b, i):
    lo, hi_ = key_range(b, i)
    return hi_ - lo + (P if i < LT else 0)


class Counted:

    def __init__(self, sem, per_layer, start):
        self.sem, self.per, self.start = sem, per_layer, start

    def at(self, layer, n):
        return layer * self.per + (n + self.start)


class Own:

    def __init__(self, eng, sem, per_layer, per_group=0):
        self.eng, self.sem, self.per, self.per_group = eng, sem, per_layer, per_group
        self.base, self.n, self.last = 0, 0, None

    def layer(self, l):
        self.base, self.n, self.last = l * self.per, 0, None

    def group(self, g):
        self.first = self.n
        self.outer = self.base
        self.base = self.base + g * self.per_group
        self.last = None

    def end_group(self):
        assert self.n - self.first == self.per_group, ("per group", self.n - self.first)
        self.n = self.first + GROUPS * self.per_group
        self.base, self.last = self.outer, None

    def end_layer(self):
        assert self.n == self.per, ("per layer", self.n)

    def step(self):
        self.n += 1
        self.last = self.sem, self.base + self.n
        return self.sem, 1

    def tell(self, sig, value):
        self.last = sig.sem, value
        return sig.sem, 1


OWN_STEPS = {"act": (7, 0), "dve": (326, 8)}


def build(nc, A):
    ctx = ExitStack()
    with ctx:
        def sb(name, shape, dt=F32):
            return ctx.enter_context(nc.sbuf_tensor(name + "_sb", shape, dt))

        def sem(name):
            return ctx.enter_context(nc.semaphore(name))

        def counted(name, per_layer, start=0):
            return Counted(sem(name), per_layer, start)

        ring = sb("ring", [P, RING, 2 * UNIT])
        x = sb("x", [P, KT, T])
        h = sb("h", [P, KT, T])
        fm = sb("fm", [P, N_FM, T])
        tmr = sb("tmr", [P, 6400])
        scr = sb("scr", [P, 5120])
        o = sb("o", [P, 2, T])
        lpa = sb("lpa", [P, N_LPA])
        lpb = sb("lpb", [P, DEPTH, N_LPB])
        lpc = sb("lpc", [P, N_LPB])
        cst = sb("cst", [P, N_CST])
        msk = sb("msk", [P, 2, LEVELS, HD], U8)
        lbs = sb("lbs", [P, DEPTH, 2 * BW])
        omlb = sb("omlb", [P, 2 * BW])
        st = sb("st", [P, 2, 2, 2, HD])
        mod = sb("mod", [P, 48, 2])
        amul = sb("amul", [P, 2, KT, 2])
        cond = sb("cond", [P, KT, 2])
        cneg = sb("cneg", [P, KT, 2])
        fg = sb("fg", [P, KT])
        eps = sb("eps", [P, 1])
        tot = sb("tot", [P, 2, 2])
        nmx = sb("nmx", [P, 3])
        sums = sb("sums", [P, 3])
        rinv = sb("rinv", [P, 3])
        vstat = sb("vstat", [P, 20])
        lt = sb("lt", [P, TILES, 20])
        rt = sb("rt", [P, 14, TILES, 4])
        comb = sb("comb", [P, TILES, GROUPS, EPG])
        cg = sb("cg", [P, TILES, EPG])
        ps = ctx.enter_context(nc.psum_tensor("ps", [P, 8, 512], F32))

        def view(tensor, at, *shape):
            n = int(np.prod(shape))
            v = tensor[:, at:at + n]
            if len(shape) == 2:
                v = v.rearrange("p (a b) -> p a b", a=shape[0])
            if len(shape) == 3:
                v = v.rearrange("p (a b c) -> p a b c", a=shape[0], b=shape[1])
            return v

        lf = view(tmr, 0, TILES, 2 * BW)
        kk = view(tmr, 2560, TILES, 2 * BW)
        hi = view(tmr, 5120, TILES, BW)
        nav = view(tmr, 0, TILES, BW)
        mv = view(tmr, 1280, TILES, BW)
        sv = view(tmr, 2560, TILES, P)
        merged = view(tmr, 0, KT, T)
        act_t = view(tmr, 0, KT, T)
        TM_DST = dict(hff=kk[:, :, 0:BW], hfb=kk[:, :, BW:2 * BW], hi=hi, nav=nav, mv=mv, sv=sv)
        lnb = view(scr, 0, 2, TILES, BW)
        osq = view(scr, 0, 2, T)
        ors = view(scr, 1280, 2, T)
        sbs = view(scr, 0, 3, T + 1)
        pts = view(scr, 1923, 2, T)
        mvsq = view(scr, 3203, TILES, BW)
        sg = view(scr, 0, 2, T)
        mt = view(scr, 1280, 2, T)
        cb = view(scr, 0, EPG, T)
        msg = view(scr, 2560, 2, T)
        nsq = view(scr, 0, 2, T)
        rs = view(scr, 1280, T)
        xn = view(scr, 1920, 2, T)
        lbraw = view(scr, 0, DEPTH, 2 * BW)
        mraw = view(scr, 4096, 2 * LEVELS, HD)

        fm_rows = fm[:, :, :].rearrange("p n t -> p (n t)")
        hgrn_scratch = [(scr, 0), (fm_rows, NAQ * T)]
        ex = [view(t, at, 2, 8, P) for t, at in hgrn_scratch]
        ke = [view(t, at + 2048, 2, LEVELS, P) for t, at in hgrn_scratch]
        kT = [view(t, at + 3840, 2, P) for t, at in hgrn_scratch]
        es = [view(t, at + 4096, BW) for t, at in hgrn_scratch]
        kd = [view(t, at + 4352, BW) for t, at in hgrn_scratch]
        at_ = [view(t, at + 4608, HEADS, P) for t, at in hgrn_scratch]

        def c(name, *shape):
            a, b = CST[name]
            return view(cst, a, *(shape or (b - a,)))

        def pa(name, *shape):
            a, b = LPA[name]
            return view(lpa, a, *(shape or (b - a,)))

        def pb(name, *shape):
            a, b = LPB[name]
            return view(lpc, a, *(shape or (b - a,)))

        nab = pa("nab", HEADS, 14 * HD)

        def slot(n):
            return ps[:, 2 * (n % 2):2 * (n % 2) + 2, :].rearrange("p b c -> p (b c)")

        def banks(b, n):
            return ps[:, b:b + n, :].rearrange("p b c -> p (b c)")

        loaded = sem("loaded")
        n_loads = 6
        params_loaded = counted("params_loaded", 32)
        arrived = [counted(f"arrived{s}", 16 * PAIRS // RING) for s in range(RING)]
        job_full = counted("job_full", JOBS)
        job_out = [counted(f"job_out{s}", JOBS // 2, 1) for s in range(2)]
        kv_out = counted("kv_out", 5 * 16)
        y_out = sem("y_out")
        lb_diff = sem("lb_diff")
        start_exp = sem("start_exp")
        cond_ready = sem("cond_ready")
        small_ready = counted("small_ready", 1)
        mod_full = counted("mod_full", 2)
        sq_ready = counted("sq_ready", 2 * KT)
        sq_used = counted("sq_used", 2 * KT)
        rs_ready = counted("rs_ready", 2)
        xn_ready = counted("xn_ready", 2 * KT)
        h_ready = counted("h_ready", 2 * KT)
        ln_in = counted("ln_in", 2)
        ln_out = counted("ln_out", 2)
        f_ready = counted("f_ready", 2)
        neg_exp = counted("neg_exp", 4)
        NU = len(HGRN_UNITS)
        decay_full = counted("decay_full", 2 * NU)
        tail_full = counted("tail_full", NU)
        ex_ready = counted("ex_ready", 2 * NU)
        es_ready = counted("es_ready", NU)
        kT_ready = counted("kT_ready", NU)
        ke_ready = counted("ke_ready", 2 * NU)
        kd_ready = counted("kd_ready", NU)
        qe_ready = counted("qe_ready", 2 * NU)
        score_full = counted("score_full", FILLS * NU)
        score_out = counted("score_out", FILLS * NU)
        o_full = counted("o_full", NU)
        s_ready = counted("s_ready", NU)
        osq_ready = counted("osq_ready", 2)
        a_done = counted("a_done", 2)
        v_stat = counted("v_stat", 1)
        v_rs = counted("v_rs", 1)
        v_ready = counted("v_ready", 1)
        NAT = len(ATT_UNITS)
        att_s_full = counted("att_s_full", NAT)
        att_s_out = counted("att_s_out", NAT)
        att_exp = counted("att_exp", NAT)
        att_rinv = counted("att_rinv", NAT)
        att_p = counted("att_p", NAT)
        att_t_full = counted("att_t_full", NAT)
        att_t_out = counted("att_t_out", NAT)
        att_o_full = counted("att_o_full", NAT)
        att_o_out = counted("att_o_out", NAT)
        m_ready = counted("m_ready", KT)
        router_full = counted("router_full", 1)
        r_in = counted("r_in", 2)
        r_exp = counted("r_exp", 2)
        cg_ready = counted("cg_ready", GROUPS)
        act_ready = counted("act_ready", GROUPS * 2 * EPG)
        start_steps = sem("start_steps")
        passed = sem("passed")
        own_sem = {e: sem(f"{e}_steps") for e in OWN_STEPS}

        block = ctx.enter_context(nc.Block())

        def out_at(l, n, g=None):
            value = job_out[n % 2].at(l, n // 2 + 1)
            return job_out[n % 2], value if g is None else value + g * (JOBS_G // 2)

        def out_of(l, n, g=None):
            sig, value = out_at(l, n, g)
            return sig.sem, value

        def full(l, n, g=None):
            return job_full.sem, job_full.at(l, n + 1 if g is None else n + 1 + g * JOBS_G)

        def alone(eng):
            eng.sem_inc(passed)

        def moe_at(kind, arg):
            return START["moe"] + [k for k, j in enumerate(PARTS["moe"]) if j.kind == kind and j.arg == arg][0]

        @block.sync
        def _(sp):
            def load(l, pair, g=None):
                n = l * PAIRS + pair if g is None else l * PAIRS + g * PAIRS_G + pair
                sp.dma_start(ring[:, pair % RING, :], A["ws"][n]).then_inc(arrived[pair % RING].sem, 16)

            def layer(l):
                for pair in range(RING, PAIRS0):
                    sp.wait_ge(job_full.sem, job_full.at(l, read_by(pair - RING)))
                    load(l, pair)
                for pair in range(PAIRS0, PAIRS0 + RING):
                    sp.wait_ge(job_full.sem, job_full.at(l, read_by(pair - RING)))
                    load(l, pair)
                with sp.Fori(0, GROUPS - 1) as g:
                    for pair in range(PAIRS0 + RING, PAIRS0 + RING + PAIRS_G):
                        sp.wait_ge(job_full.sem, job_full.at(l, read_by(pair - RING) + g * JOBS_G))
                        load(l, pair, g)
                for pair in range(PAIRS0 + RING, PAIRS0 + PAIRS_G):
                    sp.wait_ge(job_full.sem, job_full.at(l, read_by(pair - RING) + (GROUPS - 1) * JOBS_G))
                    load(l, pair + (GROUPS - 1) * PAIRS_G)

            for pair in range(RING):
                load(0, pair)
            with sp.Fori(0, DEPTH - 1) as l:
                layer(l)
                for pair in range(RING):
                    sp.wait_ge(job_full.sem, job_full.at(l, read_by(PAIRS0 + PAIRS_G + pair - RING) + (GROUPS - 1) * JOBS_G))
                    load(l + 1, pair)
            layer(DEPTH - 1)
            sp.wait_ge(h_ready.sem, h_ready.at(DEPTH, KT))
            sp.dma_start(A["y"], h[:, :, :]).then_inc(y_out, 16)
            sp.wait_ge(y_out, 16)

        @block.tensor
        def _(pe):
            def unit(x_):
                pair = x_ // 2
                return view(ring[:, pair % RING, :], (x_ % 2) * UNIT, KT, P)

            def stats(l, k):
                for kt in range(KT):
                    pe.wait_ge(sq_ready.sem, sq_ready.at(l, k * KT + kt + 1))
                    for b, lo, hi_ in ((4, 0, LAT), (5, LAT, T)):
                        mm = pe.matmul(ps[:, b, 0:hi_ - lo], c("ones"), nsq[:, kt % 2, lo:hi_],
                                       start=(kt == 0), stop=(kt == KT - 1))
                    mm.then_inc(sq_used.sem, 1)

            def product(dst, w, src, n_k):
                for k in range(n_k):
                    for lo, hi_ in ((0, LAT), (LAT, T)):
                        mm = pe.matmul(dst[:, lo:hi_], w(k), src(k, lo, hi_), start=(k == 0), stop=(k == n_k - 1))
                return mm

            arrived_pairs = set()

            def run_job(l, n, j, g=None):
                count = n // 2 if g is None else n // 2 + g * (JOBS_G // 2)
                pe.wait_ge(job_out[n % 2].sem, job_out[n % 2].at(l, count))
                for u in j.units:
                    if u // 2 not in arrived_pairs:
                        pair = u // 2
                        value = 16 * (pair // RING + 1)
                        if g is not None:
                            value = value + g * (16 * PAIRS_G // RING)
                        pe.wait_ge(arrived[pair % RING].sem, arrived[pair % RING].at(l, value))
                        arrived_pairs.add(pair)
                dst = slot(n)
                if j.kind == "ada":
                    for a in range(2):
                        w = unit(j.units[a])
                        for k in range(KT):
                            mm = pe.matmul(dst[:, 2 * a:2 * a + 2], w[:, k, :], cond[:, k, :], start=(k == 0),
                                           stop=(k == KT - 1))
                elif j.kind in ("fm", "gate", "mgate", "mup"):
                    w = unit(j.units[0])
                    mm = product(dst, lambda k: w[:, k, :], lambda k, a, b: h[:, k, a:b], KT)
                elif j.kind == "tm":
                    _, i0, i1, wide = j.arg
                    if wide == P:
                        w = unit(j.units[0])
                    else:
                        w = view(ring[:, (j.units[0] // 2) % RING, :], 0, KT, wide)
                    for i in range(i0, i1):
                        for k in range(KT):
                            mm = pe.matmul(dst[:, (i - i0) * wide:(i - i0 + 1) * wide], h[:, k, i * P:(i + 1) * P],
                                           w[:, k, :], start=(k == 0), stop=(k == KT - 1))
                elif j.kind == "onorm":
                    pe.wait_ge(osq_ready.sem, osq_ready.at(l, j.arg + 1))
                    mm = product(dst, lambda k: c("block"), lambda k, a, b: osq[:, j.arg, a:b], 1)
                elif j.kind == "rope":
                    a = j.arg
                    name = ("sk", SK) if a == SK else ("sq", a)
                    if (job_at("mix_in", "fm", name) - n) % 2:
                        pe.wait_ge(*out_of(l, job_at("mix_in", "fm", name)))
                    mm = pe.matmul(dst[:, 0:LAT], c("perm"), fm[:, a, 0:LAT], start=True, stop=True)
                elif j.kind == "mlp":
                    pe.wait_ge(v_ready.sem, v_ready.at(l, 1))
                    for gg in (2 * j.arg, 2 * j.arg + 1):
                        at = HD * (gg % 2)
                        for i in range(TILES):
                            mm = pe.matmul(dst[at:at + HD, i * P:(i + 1) * P], mv[:, i, gg * HD:(gg + 1) * HD],
                                           pa("ws", 4, P)[:, gg, :], start=True, stop=True)
                elif j.kind == "proj":
                    d, nb_ = j.arg
                    if j.arg == (0, 0):
                        pe.wait_ge(a_done.sem, a_done.at(l, 2))
                        pe.wait_ge(att_o_out.sem, att_o_out.at(l, NAT))
                    w = view(ring[:, (j.units[0] // 2) % RING, :], (j.units[0] % 2) * UNIT, NB * 2, P)
                    mm = product(dst, lambda k: w[:, 2 * nb_ + k, :],
                                 lambda k, a, b: fm[:, BRANCH_AT[nb_] + k, a:b], 2)
                elif j.kind == "out":
                    if j.arg == 0:
                        pe.wait_ge(m_ready.sem, m_ready.at(l, KT))
                    w = unit(j.units[0])
                    mm = product(dst, lambda k: w[:, k, :], lambda k, a, b: merged[:, k, a:b], KT)
                elif j.kind == "cb":
                    if j.arg == 0:
                        pe.wait_ge(cg_ready.sem, cg_ready.at(l, g + 1))
                    for i in range(TILES):
                        mm = pe.matmul(dst[:, i * P:(i + 1) * P], cg[:, i, j.arg:j.arg + 1].to_broadcast([P, P]),
                                       c("ident"), start=True, stop=True)
                elif j.kind == "down":
                    if j.arg == 0:
                        pe.wait_ge(act_ready.sem, act_ready.at(l, (g + 1) * 2 * EPG))
                    w = unit(j.units[0])
                    mm = product(dst, lambda k: w[:, k, :], lambda k, a, b: act_t[:, k, a:b], KT)
                mm.then_inc(job_full.sem, 1)

            def run_part(l, name):
                for k, j in enumerate(PARTS[name]):
                    run_job(l, START[name] + k, j)

            def free_slots(l, n):
                pe.wait_ge(*out_of(l, n - 1))
                pe.wait_ge(*out_of(l, n - 2))

            def hgrn(l):
                def decays(u, a):
                    d, stream, i = HGRN_UNITS[u]
                    if u == 0 and a == 0:
                        pe.wait_ge(f_ready.sem, f_ready.at(l, 1))
                    if u == TILES and a == 0:
                        pe.wait_ge(f_ready.sem, f_ready.at(l, 2))
                    if u >= 1:
                        pe.wait_ge(ex_ready.sem, ex_ready.at(l, 2 * (u - 1) + a + 1))
                    for b in range(2):
                        mm = pe.matmul(ps[:, 2 * a + b, :], lf[:, i, d * BW + a * P:d * BW + (a + 1) * P],
                                       c("decay", 2, 8 * P)[:, d, b * 512:(b + 1) * 512], start=True, stop=True)
                    mm.then_inc(decay_full.sem, 1)

                def tails(u):
                    d, stream, i = HGRN_UNITS[u]
                    if u >= 1:
                        pe.wait_ge(es_ready.sem, es_ready.at(l, u))
                        pe.wait_ge(kT_ready.sem, kT_ready.at(l, u))
                    pe.matmul(ps[:, 4, 0:BW], c("tail", 2, P)[:, d, :], lf[:, i, d * BW:(d + 1) * BW], start=True,
                              stop=True)
                    for a in range(2):
                        mm = pe.transpose(ps[:, 4, BW + a * P:BW + (a + 1) * P],
                                          kk[:, i, d * BW + a * P:d * BW + (a + 1) * P], c("ident"))
                    mm.then_inc(tail_full.sem, 1)

                def scores(u, f):
                    d, stream, i = HGRN_UNITS[u]
                    v = u % 2
                    if f == 0:
                        pe.wait_ge(ke_ready.sem, ke_ready.at(l, 2 * u + 2))
                        pe.wait_ge(qe_ready.sem, qe_ready.at(l, 2 * u + 2))
                    k = FILLS * u + f
                    if k >= 1:
                        pe.wait_ge(score_out.sem, score_out.at(l, k))
                    for lev in FILL_LEVELS[f]:
                        for a in range(2):
                            for par in range(2):
                                rows = slice(HD * par, HD * (par + 1))
                                if lev == LEVELS:
                                    mm = pe.matmul(ps[:, 5 + par, a * 256:a * 256 + P], kT[v][rows, a, :],
                                                   fm[rows, HQ + a, i * P:(i + 1) * P], start=True, stop=True)
                                    continue
                                half = HD >> lev
                                q = ex[v][rows, a, lev, :].rearrange("p (n two h) -> p n two h", two=2, h=half)
                                c0 = a * 256 + (lev - FILL_LEVELS[f][0]) * HD
                                mm = pe.matmul(ps[:, 5 + par, c0:c0 + HD].rearrange("p (n h) -> p n h", h=half),
                                               ke[v][rows, a, lev, :], q[:, :, 1 - d, :], start=True, stop=True)
                    mm.then_inc(score_full.sem, 1)

                def outputs(u):
                    d, stream, i = HGRN_UNITS[u]
                    v = u % 2
                    if u >= 1:
                        pe.wait_ge(s_ready.sem, s_ready.at(l, u))
                    pe.wait_ge(kd_ready.sem, kd_ready.at(l, u + 1))
                    for e in range(HEADS):
                        a, at = e // 2, HD * (e % 2)
                        pe.matmul(ps[at:at + HD, 7, 256 + a * HD:256 + (a + 1) * HD], kd[v][:, e * HD:(e + 1) * HD],
                                  hi[:, i, e * HD:(e + 1) * HD], start=True, stop=True)
                    pe.wait_ge(score_out.sem, score_out.at(l, FILLS * (u + 1)))
                    for e in range(HEADS):
                        a, at = e // 2, HD * (e % 2)
                        pe.matmul(ps[at:at + HD, 7, a * P:(a + 1) * P], hi[:, i, e * HD:(e + 1) * HD],
                                  at_[v][:, (e % 2) * 2 + e // 2, :], start=True, stop=False)
                        mm = pe.matmul(ps[at:at + HD, 7, a * P:(a + 1) * P], st[at:at + HD, d, stream, a, :],
                                       ex[v][at:at + HD, a, 7, :], start=False, stop=True)
                    mm.then_inc(o_full.sem, 1)

                pe.wait_ge(params_loaded.sem, params_loaded.at(l, 32))
                pe.wait_ge(small_ready.sem, small_ready.at(l, 1))
                tails(0)
                decays(0, 0)
                decays(0, 1)
                for u in range(NU):
                    if u + 1 < NU:
                        tails(u + 1)
                        decays(u + 1, 0)
                    scores(u, 0)
                    if u + 1 < NU:
                        decays(u + 1, 1)
                    scores(u, 1)
                    scores(u, 2)
                    outputs(u)

            def attention(l):
                def s(u):
                    b, hd, i = ATT_UNITS[u]
                    if u >= 2:
                        pe.wait_ge(att_s_out.sem, att_s_out.at(l, u - 1))
                    dst = banks(2 * (u % 2), 2)
                    if b == "na":
                        at, q, k, ck = HD * (hd % 2), NAQ + hd // 2, NAK + hd // 2, pa("nk", 2, P)[:, hd // 2, :]
                    else:
                        at, q, k, ck = HD * (hd // 2), SQ + hd % 2, SK, pa("sk")
                    lo, hi_ = key_range(b, i)
                    qs = fm[at:at + HD, q, i * P:(i + 1) * P]
                    mm = pe.matmul(dst[:, 0:hi_ - lo], qs, fm[at:at + HD, k, lo:hi_], start=True, stop=True)
                    if i < LT:
                        mm = pe.matmul(dst[:, hi_ - lo:hi_ - lo + P], qs, ck[at:at + HD, :], start=True, stop=True)
                    mm.then_inc(att_s_full.sem, 1)

                def t(u):
                    b, hd, i = ATT_UNITS[u]
                    pe.wait_ge(att_p.sem, att_p.at(l, u + 1))
                    if u >= 1:
                        pe.wait_ge(att_t_out.sem, att_t_out.at(l, u))
                    for k in range(n_keys(b, i) // P):
                        mm = pe.transpose(banks(4, 2)[:, k * P:(k + 1) * P], sbs[:, u % 3, k * P:(k + 1) * P], c("ident"))
                    mm.then_inc(att_t_full.sem, 1)

                def pv(u):
                    b, hd, i = ATT_UNITS[u]
                    pe.wait_ge(att_t_out.sem, att_t_out.at(l, u + 1))
                    if u >= 2:
                        pe.wait_ge(att_o_out.sem, att_o_out.at(l, u - 1))
                    lo, hi_ = key_range(b, i)
                    if b == "na":
                        at, v, cv, cols = HD * (hd % 2), nav, pa("nv"), slice(hd * HD, (hd + 1) * HD)
                    else:
                        at, v, cv, cols = HD * (hd // 2), sv, pa("sv"), slice((hd // 2) * HD, (hd // 2 + 1) * HD)
                    n = n_keys(b, i) // P
                    for k in range(n):
                        w = cv[:, cols] if lo + k * P >= hi_ else v[:, lo // P + k, cols]
                        mm = pe.matmul(ps[at:at + HD, 6 + u % 2, 0:P], w, pts[:, u % 2, k * P:(k + 1) * P],
                                       start=(k == 0), stop=(k == n - 1))
                    mm.then_inc(att_o_full.sem, 1)

                for step in range(-2, NAT + 1):
                    if step + 2 < NAT:
                        s(step + 2)
                    if 0 <= step - 1:
                        pv(step - 1)
                    if 0 <= step < NAT:
                        t(step)

            def router(l):
                for i in range(TILES):
                    for k in range(KT):
                        if i == 0:
                            pe.wait_ge(h_ready.sem, h_ready.at(l, KT + k + 1))
                        mm = pe.matmul(ps[:, 6, i * 20:(i + 1) * 20], h[:, k, i * P:(i + 1) * P],
                                       pb("wr", KT, 20)[:, k, :], start=(k == 0), stop=(k == KT - 1))
                mm.then_inc(router_full.sem, 1)

            pe.wait_ge(loaded, 16 * n_loads)
            pe.wait_ge(cond_ready, 1)
            with pe.Fori(0, DEPTH) as l:
                arrived_pairs.clear()
                stats(l, 0)
                run_part(l, "ada")
                pe.wait_ge(h_ready.sem, h_ready.at(l, KT))
                run_part(l, "hgrn_in")
                free_slots(l, START["hgrn_out"])
                hgrn(l)
                run_part(l, "hgrn_out")
                run_part(l, "mix_in")
                free_slots(l, START["merge"])
                attention(l)
                run_part(l, "merge")
                run_part(l, "out")
                stats(l, 1)
                router(l)
                seen = set(arrived_pairs)
                with pe.Fori(0, GROUPS) as g:
                    arrived_pairs.clear()
                    for k, j in enumerate(PARTS["moe"]):
                        run_job(l, START["moe"] + k, j, g)
                arrived_pairs |= seen
            stats(DEPTH, 0)

        @block.scalar
        def _(act):
            own = Own(act, own_sem["act"], *OWN_STEPS["act"])
            for dst, src in ((cond[:, :, :], A["cT"]), (x[:, :, :], A["xT"]), (cst[:, :], A["cst"]),
                             (lpb[:, :, :], A["lpb"]), (mraw, A["msk"]), (fg[:, :], A["fg"])):
                act.dma_start(dst, src).then_inc(loaded, 16)
            act.dma_start(lbraw, A["lbr"]).then_inc(lb_diff, 16)
            act.wait_ge(loaded, 16 * n_loads)
            act.activation(cneg[:, :, :], cond[:, :, :], ACT.Exp, scale=-1.0).then_inc(start_exp, 1)
            act.wait_ge(lb_diff, 17)
            act.activation(lbs[:, 1, :], lbs[:, 1, :], ACT.Exp).then_inc(start_exp, 1)
            act.wait_ge(cond_ready, 1)

            def norm(l, k):
                for kt in range(KT):
                    if k == 1:
                        act.wait_ge(*out_of(l, job_at("out", "out", kt)))
                    elif kt == 0:
                        for s in range(2):
                            act.wait_ge(job_out[s].sem, job_out[s].at(l, 0))
                    if kt >= 2:
                        act.wait_ge(sq_used.sem, sq_used.at(l, k * KT + kt - 1))
                    act.activation(nsq[:, kt % 2, :], x[:, kt, :], ACT.Square).then_inc(sq_ready.sem, 1)
                act.wait_ge(sq_used.sem, sq_used.at(l, (k + 1) * KT))
                act.activation(rs, banks(4, 2)[:, 0:T], ACT.Ln, bias=eps[:, 0:1], scale=1.0 / D).then_inc(*own.step())
                act.wait_ge(*own.last)
                act.activation(rs, rs, ACT.Exp, scale=-0.5).then_inc(*own.tell(rs_ready, rs_ready.at(l, k + 1)))

            def modulate(l, k):
                act.wait_ge(mod_full.sem, mod_full.at(l, k + 1))
                for kt in range(KT):
                    act.wait_ge(xn_ready.sem, xn_ready.at(l, k * KT + kt + 1))
                    for w, lo, hi_ in ((0, 0, LAT), (1, LAT, T)):
                        ins = act.activation(h[:, kt, lo:hi_], xn[:, kt % 2, lo:hi_], ACT.Identity,
                                             bias=mod[:, 24 * k + kt, w:w + 1], scale=amul[:, k, kt, w:w + 1])
                    ins.then_inc(h_ready.sem, 1)

            def run_job(l, n, j, g=None):
                src = slot(n)[:, 0:T]
                if j.kind == "fm":
                    name, dst, _ = j.arg
                    act.wait_ge(*full(l, n))
                    if name in ("hq", "hog"):
                        act.activation(fm[:, dst, :], src, ACT.Exp, scale=-1.0).then_inc(neg_exp.sem, 1)
                        return
                    scale = HD ** -0.5 if name in ("naq", "sq") else 1.0
                    act.activation(fm[:, dst, :], src, ACT.Copy, scale=scale).then_inc(job_out[n % 2].sem, 1)
                elif j.kind == "tm":
                    name, i0, i1, wide = j.arg
                    act.wait_ge(*full(l, n))
                    if name == "nav" and i0 == 0:
                        act.wait_ge(o_full.sem, o_full.at(l, NU))
                    src = slot(n)[:, 0:(i1 - i0) * wide].rearrange("p (i w) -> p i w", w=wide)
                    fn, scale = (ACT.Exp, -1.0) if name in ("hff", "hfb") else (ACT.Copy, 1.0)
                    act.activation(TM_DST[name][:, i0:i1, :], src, fn, scale=scale).then_inc(job_out[n % 2].sem, 1)
                elif j.kind == "gate":
                    d, nb_ = j.arg
                    act.wait_ge(*full(l, n))
                    k = 4 * d + nb_
                    if k >= 2:
                        act.wait_ge(*out_of(l, job_at("merge", "proj", ((k - 2) // 4, (k - 2) % 4))))
                    act.activation(sg[:, nb_ % 2, :], src, ACT.Sigmoid).then_inc(job_out[n % 2].sem, 1)
                elif j.kind == "cb":
                    act.wait_ge(*full(l, n, g))
                    act.activation(cb[:, j.arg, :], src, ACT.Copy).then_inc(job_out[n % 2].sem, 1)
                elif j.kind == "mgate":
                    e, ft = j.arg
                    act.wait_ge(*full(l, n, g))
                    k = 2 * e + ft
                    if k >= 2:
                        act.wait_ge(*out_of(l, moe_at("mup", ((k - 2) // 2, (k - 2) % 2)), g))
                    act.activation(msg[:, ft, :], src, ACT.Silu).then_inc(job_out[n % 2].sem, 1)

            def logs(l, d):
                act.wait_ge(ln_in.sem, ln_in.at(l, d + 1))
                act.activation(lnb[:, d, :, :], lnb[:, d, :, :], ACT.Ln).then_inc(*own.step())
                v = lf[:, :, d * BW:(d + 1) * BW]
                act.activation(v, v, ACT.Ln).then_inc(ln_out.sem, 1)

            def hgrn(l):
                for u in range(NU):
                    v = u % 2
                    if u >= 2:
                        act.wait_ge(o_full.sem, o_full.at(l, u - 1))
                    for a in range(2):
                        act.wait_ge(decay_full.sem, decay_full.at(l, 2 * u + a + 1))
                        act.activation(ex[v][:, a, :, :], banks(2 * a, 2).rearrange("p (k t) -> p k t", k=8),
                                       ACT.Exp).then_inc(ex_ready.sem, 1)
                        if a == 0:
                            act.wait_ge(kT_ready.sem, kT_ready.at(l, u + 1))
                            act.activation(es[v], ps[:, 4, 0:BW], ACT.Exp).then_inc(es_ready.sem, 1)
                act.wait_ge(s_ready.sem, s_ready.at(l, NU))
                act.dma_start(A["st_out"][l], st[:, :, 0, :, :]).then_inc(kv_out.sem, 16)

            def hgrn_norm(l):
                act.wait_ge(o_full.sem, o_full.at(l, NU))
                for a in range(2):
                    act.activation(osq[:, a, :], o[:, a, :], ACT.Square).then_inc(osq_ready.sem, 1)
                for a in range(2):
                    n = START["hgrn_out"] + a
                    act.wait_ge(*full(l, n))
                    act.activation(ors[:, a, :], slot(n)[:, 0:T], ACT.Ln, bias=eps[:, 0:1], scale=1.0 / HD).then_inc(*own.step())
                    act.wait_ge(*own.last)
                    act.activation(ors[:, a, :], ors[:, a, :], ACT.Exp, scale=-0.5).then_inc(job_out[n % 2].sem, 1)

            def attention(l):
                for step in range(-2, NAT + 1):
                    u = step + 1
                    if 0 <= u < NAT:
                        b, hd, i = ATT_UNITS[u]
                        n = n_keys(b, i) + (b == "swa")
                        act.wait_ge(att_s_out.sem, att_s_out.at(l, u + 1))
                        if u >= 3:
                            act.wait_ge(att_rinv.sem, att_rinv.at(l, u - 2))
                        act.activation(sbs[:, u % 3, 0:n], sbs[:, u % 3, 0:n], ACT.Exp, bias=nmx[:, u % 3:u % 3 + 1],
                                       accum_out=sums[:, u % 3:u % 3 + 1]).then_inc(att_exp.sem, 1)
                    u = step
                    if 0 <= u < NAT:
                        b, hd, i = ATT_UNITS[u]
                        act.wait_ge(att_t_full.sem, att_t_full.at(l, u + 1))
                        if u >= 2:
                            act.wait_ge(att_o_full.sem, att_o_full.at(l, u - 1))
                        n = n_keys(b, i)
                        act.activation(pts[:, u % 2, 0:n], banks(4, 2)[:, 0:n], ACT.Copy).then_inc(att_t_out.sem, 1)

            with act.Fori(0, DEPTH) as l:
                own.layer(l)
                norm(l, 0)
                act.dma_start(lpa[:, :], A["lpa"][l]).then_inc(params_loaded.sem, 16)
                act.dma_start(st[:, :, 1, :, :], A["st_in"][l]).then_inc(params_loaded.sem, 16)
                modulate(l, 0)
                for k, j in enumerate(PARTS["hgrn_in"]):
                    run_job(l, START["hgrn_in"] + k, j)
                    if j.kind == "tm" and j.arg[0:2] == ("hi", LT):
                        logs(l, 0)
                        logs(l, 1)
                act.wait_ge(f_ready.sem, f_ready.at(l, 2))
                hgrn(l)
                hgrn_norm(l)
                for k, j in enumerate(PARTS["mix_in"]):
                    run_job(l, START["mix_in"] + k, j)
                    if j.kind == "tm" and j.arg[0:2] == ("mv", LT):
                        act.wait_ge(v_stat.sem, v_stat.at(l, 1))
                        act.activation(vstat[:, :], vstat[:, :], ACT.Ln, bias=eps[:, 0:1], scale=1.0 / HD).then_inc(*own.step())
                        act.wait_ge(*own.last)
                        act.activation(vstat[:, :], vstat[:, :], ACT.Exp, scale=-0.5).then_inc(v_rs.sem, 1)
                kv_jobs = [job_at("mix_in", "fm", t) for t in (("sk", SK), ("nak", NAK), ("nak", NAK + 1))]
                kv_jobs += [job_at("mix_in", "tm", (t, LT)) for t in ("nav", "sv")]
                act.wait_ge(*out_of(l, max(n for n in kv_jobs if n % 2 == 0)))
                act.wait_ge(*out_of(l, max(n for n in kv_jobs if n % 2 == 1)))
                act.dma_start(A["nk_out"][l], fm[:, NAK:NAK + 2, LAT:T]).then_inc(kv_out.sem, 16)
                act.dma_start(A["nv_out"][l], nav[:, CT, :]).then_inc(kv_out.sem, 16)
                act.dma_start(A["sk_out"][l], fm[:, SK, LAT:T]).then_inc(kv_out.sem, 16)
                act.dma_start(A["sv_out"][l], sv[:, CT, :]).then_inc(kv_out.sem, 16)
                attention(l)
                for k, j in enumerate(PARTS["merge"]):
                    run_job(l, START["merge"] + k, j)
                norm(l, 1)
                modulate(l, 1)
                for k in range(2):
                    act.wait_ge(r_in.sem, r_in.at(l, k + 1))
                    v = rt[:, 12 + k, :, 0:4 if k == 0 else 1]
                    act.activation(v, v, ACT.Exp).then_inc(r_exp.sem, 1)
                with act.Fori(0, GROUPS) as g:
                    for k, j in enumerate(PARTS["moe"]):
                        run_job(l, START["moe"] + k, j, g)
                own.end_layer()
            own.layer(DEPTH)
            norm(DEPTH, 0)
            for kt in range(KT):
                act.wait_ge(xn_ready.sem, xn_ready.at(DEPTH, kt + 1))
                act.activation(h[:, kt, :], xn[:, kt % 2, :], ACT.Copy, scale=fg[:, kt:kt + 1])\
                   .then_inc(h_ready.sem, 1)
            act.wait_ge(kv_out.sem, kv_out.at(DEPTH, 0))

        @block.vector
        def _(dve):
            own = Own(dve, own_sem["dve"], *OWN_STEPS["dve"])
            own.layer(0)
            head = start_steps
            n_head = [0]

            def first(ins):
                n_head[0] += 1
                ins.then_inc(head, 1)
                dve.wait_ge(head, n_head[0])

            for s in range(2):
                dve.sem_inc(job_out[s].sem)
            dve.memset(eps[:, :], EPS).then_inc(head, 1)
            n_head[0] += 1
            dve.wait_ge(lb_diff, 16)
            dve.tensor_tensor(lbs[:, 1, :], lbraw[:, 0, :], lbraw[:, 1, :], ALU.subtract).then_inc(lb_diff, 1)
            dve.memset(lbs[:, 0, :], 0.0).then_inc(head, 1)
            n_head[0] += 1
            dve.wait_ge(start_exp, 2)
            first(dve.tensor_scalar(lbs[:, 1, :], lbs[:, 1, :], 1.0, None, ALU.add))
            first(dve.reciprocal(lbs[:, 1, :], lbs[:, 1, :]))
            first(dve.tensor_scalar(cneg[:, :, :], cneg[:, :, :], 1.0, None, ALU.add))
            first(dve.reciprocal(cneg[:, :, :], cneg[:, :, :]))
            dve.tensor_tensor(cond[:, :, :], cond[:, :, :], cneg[:, :, :], ALU.mult).then_inc(cond_ready, 1)


            def norm_x(l, k):
                dve.wait_ge(rs_ready.sem, rs_ready.at(l, k + 1))
                for kt in range(KT):
                    if kt >= 2:
                        dve.wait_ge(h_ready.sem, h_ready.at(l, k * KT + kt - 1))
                    dve.tensor_tensor(xn[:, kt % 2, :], x[:, kt, :], rs, ALU.mult).then_inc(*own.tell(xn_ready, xn_ready.at(l, k * KT + kt + 1)))

            def gain(l, k):
                name = ("n1", "n2")[k]
                dve.wait_ge(*own.last)
                g = pb(name).unsqueeze(2).to_broadcast([P, KT, 2])
                dve.scalar_tensor_tensor(out=amul[:, k, :, :], in0=mod[:, 24 * k + 8:24 * k + 16, :],
                                                  scalar=1.0, in1=g, op0=ALU.add, op1=ALU.mult).then_inc(*own.tell(mod_full, mod_full.at(l, k + 1)))

            def residual(l, n, g, d, first_unit):
                for w, lo, hi_ in ((0, 0, LAT), (1, LAT, T)):
                    ins = dve.scalar_tensor_tensor(
                        out=x[:, d, lo:hi_], in0=slot(n)[:, lo:hi_], scalar=mod[:, first_unit + d, w:w + 1],
                        in1=x[:, d, lo:hi_], op0=ALU.mult, op1=ALU.add)
                    if w == 0:
                        ins.then_inc(*own.step())
                ins.then_inc(*own.tell(*out_at(l, n, g)))

            def run_job(l, n, j, g=None):
                src = slot(n)[:, 0:T]
                if j.kind == "ada":
                    i = j.arg
                    dve.wait_ge(*full(l, n))
                    b = pb("b_ada")[:, 2 * i:2 * i + 2].unsqueeze(2).to_broadcast([P, 2, 2])
                    dve.tensor_tensor(mod[:, 2 * i:2 * i + 2, :], slot(n)[:, 0:4].rearrange("p (u w) -> p u w", w=2), b, ALU.add).then_inc(*own.tell(*out_at(l, n)))
                    if i == 7:
                        gain(l, 0)
                    if i == 19:
                        gain(l, 1)
                elif j.kind == "fm" and j.arg[0] in ("hq", "hog"):
                    name, dst, _ = j.arg
                    k = (dst - HQ if name == "hq" else 2 + dst - HOG)
                    dve.wait_ge(neg_exp.sem, neg_exp.at(l, k + 1))
                    v = fm[:, dst, :]
                    dve.tensor_scalar(v, v, 1.0, None, ALU.add).then_inc(*own.step())
                    dve.wait_ge(*own.last)
                    dve.reciprocal(v, v).then_inc(*own.step())
                    dve.wait_ge(*own.last)
                    dve.tensor_tensor(v, v, src, ALU.mult).then_inc(*own.tell(*out_at(l, n)))
                elif j.kind == "rope":
                    a = j.arg
                    v = fm[:, a, 0:LAT]
                    dve.wait_ge(*full(l, n))
                    dve.tensor_tensor(v, v, c("cos"), ALU.mult).then_inc(*own.step())
                    dve.tensor_tensor(slot(n)[:, 0:LAT], slot(n)[:, 0:LAT], c("sin"), ALU.mult).then_inc(*own.step())
                    dve.wait_ge(*own.last)
                    dve.tensor_tensor(v, v, slot(n)[:, 0:LAT], ALU.add).then_inc(*own.tell(*out_at(l, n)))
                elif j.kind == "mlp":
                    a = j.arg
                    dve.wait_ge(*full(l, n))
                    dve.wait_ge(*out_of(l, job_at("mix_in", "fm", ("mu", MU + a))))
                    b = pa("smb", 2, P)[:, a, :].unsqueeze(1).to_broadcast([P, TILES, P])
                    s3 = src.rearrange("p (i t) -> p i t", t=P)
                    dve.tensor_tensor(s3, s3, b, ALU.add).then_inc(*own.step())
                    dve.wait_ge(*own.last)
                    dve.tensor_tensor(fm[:, MU + a, :], fm[:, MU + a, :], src, ALU.mult).then_inc(*own.tell(*out_at(l, n)))
                elif j.kind == "proj":
                    d, nb_ = j.arg
                    dve.wait_ge(*full(l, n))
                    dve.wait_ge(*out_of(l, n - 1))
                    if nb_ == 0:
                        dve.tensor_tensor(merged[:, d, :], src, sg[:, 0, :], ALU.mult).then_inc(*own.tell(*out_at(l, n)))
                        return
                    dve.tensor_tensor(mt[:, nb_ % 2, :], src, sg[:, nb_ % 2, :], ALU.mult).then_inc(*own.tell(*out_at(l, n)))
                    dve.wait_ge(*own.last)
                    dve.tensor_tensor(merged[:, d, :], merged[:, d, :], mt[:, nb_ % 2, :], ALU.add)\
                       .then_inc(*(own.tell(m_ready, m_ready.at(l, d + 1)) if nb_ == NB - 1 else own.step()))
                elif j.kind == "out":
                    dve.wait_ge(*full(l, n))
                    residual(l, n, None, j.arg, 16)
                elif j.kind == "mup":
                    e, ft = j.arg
                    dve.wait_ge(*full(l, n, g))
                    dve.wait_ge(*out_of(l, n - 1, g))
                    dve.tensor_tensor(act_t[:, 2 * e + ft, :], src, msg[:, ft, :], ALU.mult).then_inc(*own.tell(*out_at(l, n, g)))
                elif j.kind == "down":
                    dve.wait_ge(*full(l, n, g))
                    dve.wait_ge(*own.last)
                    residual(l, n, g, j.arg, 40)

            def forget(l, d):
                n = job_at("hgrn_in", "tm", (("hff", "hfb")[d], LT))
                dve.wait_ge(*out_of(l, n))
                dve.wait_ge(*out_of(l, n - 1))
                cols = slice(d * BW, (d + 1) * BW)
                k, f, b = kk[:, :, cols], lf[:, :, cols], lnb[:, d, :, :]
                wide = [P, TILES, BW]
                dve.tensor_scalar(k, k, 1.0, None, ALU.add).then_inc(*own.step())
                dve.wait_ge(*own.last)
                dve.reciprocal(k, k).then_inc(*own.step())
                dve.wait_ge(*own.last)
                dve.tensor_tensor(f, k, omlb[:, cols].unsqueeze(1).to_broadcast(wide), ALU.mult).then_inc(*own.step())
                dve.wait_ge(*own.last)
                dve.tensor_tensor(f, f, lbs[:, l, cols].unsqueeze(1).to_broadcast(wide), ALU.add).then_inc(*own.step())
                dve.wait_ge(*own.last)
                dve.tensor_scalar(k, f, -1.0, 1.0, ALU.mult, ALU.add).then_inc(*own.step())
                dve.tensor_scalar(b, f, LN_SPLIT, 1.0, ALU.mult, ALU.min).then_inc(*own.step())
                dve.wait_ge(*own.last)
                dve.tensor_scalar(b, b, TINY * LN_SPLIT, None, ALU.max).then_inc(*own.step())
                dve.tensor_scalar(f, f, 1.0 / LN_SPLIT, None, ALU.max).then_inc(*own.tell(ln_in, ln_in.at(l, d + 1)))

            def hgrn(l):
                def keys(u):
                    dve.wait_ge(tail_full.sem, tail_full.at(l, u + 1))
                    if u >= 2:
                        dve.wait_ge(o_full.sem, o_full.at(l, u - 1))
                    dve.tensor_copy(kT[u % 2], ps[:, 4, BW:2 * BW].rearrange("p (a s) -> p a s", a=2)).then_inc(*own.tell(kT_ready, kT_ready.at(l, u + 1)))
                    if u % TILES < 2:
                        dve.memset(at_[u % 2], 0.0).then_inc(*own.step())

                def queries(u, a):
                    d, stream, i = HGRN_UNITS[u]
                    v = u % 2
                    dve.wait_ge(ke_ready.sem, ke_ready.at(l, 2 * u + a + 1))
                    last = 127 if d == 0 else 0
                    dve.tensor_copy(tot[:, v, a:a + 1], ex[v][:, a, 7, last:last + 1]).then_inc(*own.step())
                    dve.wait_ge(*own.last)
                    q = fm[:, HQ + a, i * P:(i + 1) * P].unsqueeze(1).to_broadcast([P, 8, P])
                    dve.tensor_tensor(ex[v][:, a, :, :], ex[v][:, a, :, :], q, ALU.mult).then_inc(*own.tell(qe_ready, qe_ready.at(l, 2 * u + a + 1)))

                def take_scores(u, f):
                    d, stream, i = HGRN_UNITS[u]
                    v = u % 2
                    k = FILLS * u + f
                    dve.wait_ge(*own.last)
                    dve.wait_ge(score_full.sem, score_full.at(l, k + 1))
                    alone(dve)
                    both = banks(5, 2).rearrange("p (e c) -> p e c", e=HEADS)
                    for lev in FILL_LEVELS[f]:
                        if lev != FILL_LEVELS[f][0]:
                            dve.wait_ge(*own.last)
                            alone(dve)
                        if lev == LEVELS:
                            m = c("ident").bitcast(mybir.dt.int32).unsqueeze(1).to_broadcast([P, HEADS, P])
                            ins = dve.copy_predicated(at_[v], m, both[:, :, 0:P])
                        else:
                            half = HD >> lev
                            dst = at_[v].rearrange("p e (n two h) -> p e n two h", two=2, h=half)[:, :, :, 1 - d, :]
                            m = msk[:, d, lev, :].rearrange("p (n h) -> p n h", h=half).unsqueeze(1)\
                                .to_broadcast([P, HEADS, HD // half, half])
                            c0 = (lev - FILL_LEVELS[f][0]) * HD
                            ins = dve.copy_predicated(dst, m, both[:, :, c0:c0 + HD].rearrange(
                                "p e (n h) -> p e n h", h=half))
                        if lev == FILL_LEVELS[f][-1]:
                            ins.then_inc(*own.tell(score_out, score_out.at(l, k + 1)))
                        else:
                            ins.then_inc(*own.step())

                def results(u):
                    d, stream, i = HGRN_UNITS[u]
                    dve.wait_ge(o_full.sem, o_full.at(l, u + 1))
                    src = ps[:, 7, 0:BW].rearrange("p (a t) -> p a t", a=2)
                    dst = o[:, :, i * P:(i + 1) * P]
                    if d == 0:
                        dve.tensor_copy(dst, src).then_inc(*own.step())
                    else:
                        dve.tensor_tensor(dst, dst, src, ALU.add).then_inc(*own.step())
                    for a in range(2):
                        ins = dve.scalar_tensor_tensor(
                            out=st[:, d, stream, a, :], in0=st[:, d, stream, a, :], scalar=tot[:, u % 2, a:a + 1],
                            in1=ps[:, 7, 256 + a * HD:256 + (a + 1) * HD], op0=ALU.mult, op1=ALU.add)
                        if a == 0:
                            ins.then_inc(*own.step())
                    ins.then_inc(*own.tell(s_ready, s_ready.at(l, u + 1)))

                keys(0)
                queries(0, 0)
                queries(0, 1)
                for u in range(NU):
                    if u + 1 < NU:
                        keys(u + 1)
                    take_scores(u, 0)
                    take_scores(u, 1)
                    take_scores(u, 2)
                    if u + 1 < NU:
                        queries(u + 1, 0)
                        queries(u + 1, 1)
                    results(u)

            def hgrn_norm(l):
                for a in range(2):
                    dve.wait_ge(*out_of(l, START["hgrn_out"] + a))
                    v = o[:, a, :]
                    dve.tensor_tensor(v, v, ors[:, a, :], ALU.mult).then_inc(*own.step())
                    dve.wait_ge(*own.last)
                    dve.scalar_tensor_tensor(out=fm[:, HQ + a, :], in0=v, scalar=pb("on")[:, a:a + 1],
                                                      in1=fm[:, HOG + a, :], op0=ALU.mult, op1=ALU.mult).then_inc(*own.tell(a_done, a_done.at(l, a + 1)))

            def mlp_norm(l):
                dve.wait_ge(*out_of(l, job_at("mix_in", "tm", ("mv", 0))))
                dve.wait_ge(*out_of(l, job_at("mix_in", "tm", ("mv", LT))))
                dve.tensor_tensor(mvsq, mv, mv, ALU.mult).then_inc(*own.step())
                dve.wait_ge(*own.last)
                dve.tensor_reduce(vstat[:, :], mvsq.rearrange("p i (g c) -> p (i g) c", c=HD), AX.X, ALU.add).then_inc(*own.tell(v_stat, v_stat.at(l, 1)))
                dve.wait_ge(v_rs.sem, v_rs.at(l, 1))
                v = mv.rearrange("p i (g c) -> p (i g) c", c=HD)
                dve.tensor_tensor(v, v, vstat[:, :].unsqueeze(2).to_broadcast([P, 20, HD]), ALU.mult).then_inc(*own.tell(v_ready, v_ready.at(l, 1)))

            def attention(l):
                for step in range(-2, NAT + 1):
                    u = step + 2
                    if u < NAT:
                        b, hd, i = ATT_UNITS[u]
                        lo, hi_ = key_range(b, i)
                        n = hi_ - lo
                        dve.wait_ge(att_s_full.sem, att_s_full.at(l, u + 1))
                        if u >= 3:
                            dve.wait_ge(att_t_full.sem, att_t_full.at(l, u - 2))
                        src, dst = banks(2 * (u % 2), 2), sbs[:, u % 3, :]
                        if i == CT:
                            dve.tensor_copy(dst[:, 0:n], src[:, 0:n]).then_inc(*own.step())
                        else:
                            if b == "na":
                                e0 = (6 - 2 * i) * HD
                                bias = nab[:, hd, e0:e0 + LAT]
                            else:
                                m0 = P if i == 0 else 0
                                bias = c("swm")[:, m0:m0 + n]
                            dve.tensor_tensor(dst[:, 0:n], src[:, 0:n], bias, ALU.add).then_inc(*own.step())
                            dve.tensor_copy(dst[:, n:n + P], src[:, n:n + P]).then_inc(*own.step())
                            n += P
                        if b == "swa":
                            dve.tensor_copy(dst[:, n:n + 1], pa("sink")[:, hd:hd + 1]).then_inc(*own.step())
                            n += 1
                        dve.wait_ge(*own.last)
                        dve.tensor_reduce(nmx[:, u % 3:u % 3 + 1], dst[:, 0:n], AX.X, ALU.max, negate=True).then_inc(*own.tell(att_s_out, att_s_out.at(l, u + 1)))
                    u = step + 1
                    if 0 <= u < NAT:
                        dve.wait_ge(att_exp.sem, att_exp.at(l, u + 1))
                        if u >= 3:
                            dve.wait_ge(att_p.sem, att_p.at(l, u - 2))
                        dve.reciprocal(rinv[:, u % 3:u % 3 + 1], sums[:, u % 3:u % 3 + 1]).then_inc(*own.tell(att_rinv, att_rinv.at(l, u + 1)))
                    u = step - 1
                    if 0 <= u:
                        b, hd, i = ATT_UNITS[u]
                        at, q = (HD * (hd % 2), NAQ + hd // 2) if b == "na" else (HD * (hd // 2), SQ + hd % 2)
                        dve.wait_ge(att_o_full.sem, att_o_full.at(l, u + 1))
                        dve.tensor_copy(fm[at:at + HD, q, i * P:(i + 1) * P], ps[at:at + HD, 6 + u % 2, 0:P]).then_inc(*own.tell(att_o_out, att_o_out.at(l, u + 1)))

            def first_of(dst, eq, tk):
                dve.wait_ge(*own.last)
                dve.tensor_copy(dst[:, :, 0:1], eq[:, :, 0:1]).then_inc(*own.step())
                dve.tensor_copy(tk[:, :, 0:1], eq[:, :, 0:1]).then_inc(*own.step())
                for j in range(1, 4):
                    dve.wait_ge(*own.last)
                    dve.tensor_tensor(dst[:, :, j:j + 1], eq[:, :, j:j + 1], tk[:, :, j - 1:j], ALU.is_gt).then_inc(*own.step())
                    if j < 3:
                        dve.tensor_tensor(tk[:, :, j:j + 1], eq[:, :, j:j + 1], tk[:, :, j - 1:j], ALU.max).then_inc(*own.step())

            def router(l):
                four = [P, TILES, 4]

                def row(k):
                    return rt[:, k, :, :]

                def col(k):
                    return rt[:, 11, :, k:k + 1]
                eq, tk, og, esel, oh1, oh2, es2, ce, tmp = (row(k) for k in range(9))
                gm, gs, m1, m2 = (col(k) for k in range(4))
                gex, dlt = rt[:, 12, :, :], rt[:, 13, :, 0:1]
                w1, w2 = rt[:, 10, :, 0:1], rt[:, 10, :, 1:2]
                dve.wait_ge(router_full.sem, router_full.at(l, 1))
                dve.tensor_tensor(lt[:, :, :], ps[:, 6, 0:100].rearrange("p (i e) -> p i e", e=20), pb("rb").unsqueeze(1).to_broadcast([P, TILES, 20]), ALU.add).then_inc(*own.step())
                dve.wait_ge(*own.last)
                g4 = lt[:, :, 0:4]
                dve.tensor_reduce(gm, g4, AX.X, ALU.max).then_inc(*own.step())
                dve.wait_ge(*own.last)
                dve.tensor_tensor(eq, g4, gm.to_broadcast(four), ALU.is_equal).then_inc(*own.step())
                dve.tensor_tensor(gex, g4, gm.to_broadcast(four), ALU.subtract).then_inc(*own.tell(r_in, r_in.at(l, 1)))
                first_of(og, eq, tk)
                dve.wait_ge(*own.last)
                for g in range(GROUPS):
                    e4 = lt[:, :, 4 + 4 * g:8 + 4 * g]
                    if g == 0:
                        dve.tensor_tensor(esel, e4, og[:, :, 0:1].to_broadcast(four), ALU.mult).then_inc(*own.step())
                        continue
                    dve.tensor_tensor(tmp, e4, og[:, :, g:g + 1].to_broadcast(four), ALU.mult).then_inc(*own.step())
                    dve.wait_ge(*own.last)
                    dve.tensor_tensor(esel, esel, tmp, ALU.add).then_inc(*own.step())
                    dve.wait_ge(*own.last)
                dve.tensor_reduce(m1, esel, AX.X, ALU.max).then_inc(*own.step())
                dve.wait_ge(*own.last)
                dve.tensor_tensor(eq, esel, m1.to_broadcast(four), ALU.is_equal).then_inc(*own.step())
                first_of(oh1, eq, tk)
                dve.wait_ge(*own.last)
                dve.scalar_tensor_tensor(out=es2, in0=oh1, scalar=NEG, in1=esel, op0=ALU.mult, op1=ALU.add).then_inc(*own.step())
                dve.wait_ge(*own.last)
                dve.tensor_reduce(m2, es2, AX.X, ALU.max).then_inc(*own.step())
                dve.wait_ge(*own.last)
                dve.tensor_tensor(dlt, m2, m1, ALU.subtract).then_inc(*own.tell(r_in, r_in.at(l, 2)))
                dve.tensor_tensor(eq, es2, m2.to_broadcast(four), ALU.is_equal).then_inc(*own.step())
                first_of(oh2, eq, tk)
                dve.wait_ge(r_exp.sem, r_exp.at(l, 2))
                dve.tensor_reduce(gs, gex, AX.X, ALU.add).then_inc(*own.step())
                dve.tensor_scalar(w1, dlt, 1.0, None, ALU.add).then_inc(*own.step())
                dve.wait_ge(*own.last)
                dve.tensor_tensor(w1, w1, gs, ALU.mult).then_inc(*own.step())
                dve.wait_ge(*own.last)
                dve.reciprocal(w1, w1).then_inc(*own.step())
                dve.wait_ge(*own.last)
                dve.tensor_tensor(w2, w1, dlt, ALU.mult).then_inc(*own.step())
                dve.tensor_tensor(oh1, oh1, w1.to_broadcast(four), ALU.mult).then_inc(*own.step())
                dve.wait_ge(*own.last)
                dve.tensor_tensor(oh2, oh2, w2.to_broadcast(four), ALU.mult).then_inc(*own.step())
                dve.wait_ge(*own.last)
                dve.tensor_tensor(ce, oh1, oh2, ALU.add).then_inc(*own.step())
                dve.wait_ge(*own.last)
                for g in range(GROUPS):
                    dve.tensor_tensor(comb[:, :, g, :], ce, og[:, :, g:g + 1].to_broadcast(four), ALU.mult).then_inc(*own.step())
                dve.wait_ge(*own.last)
                alone(dve)

            dve.wait_ge(loaded, 16 * n_loads)
            first(dve.tensor_copy(msk[:, :, :, :].rearrange("p d l t -> p (d l) t"), mraw))
            with dve.Fori(0, DEPTH) as l:
                own.layer(l)
                dve.tensor_copy(lpc[:, :], lpb[:, l, :]).then_inc(*own.step())
                dve.tensor_scalar(omlb[:, :], lbs[:, l, :], -1.0, 1.0, ALU.mult, ALU.add).then_inc(*own.step())
                dve.memset(st[:, :, 0, :, :], 0.0).then_inc(*own.tell(small_ready, small_ready.at(l, 1)))
                dve.wait_ge(*own.last)
                for k, j in enumerate(PARTS["ada"]):
                    run_job(l, START["ada"] + k, j)
                norm_x(l, 0)
                dve.wait_ge(h_ready.sem, h_ready.at(l, KT))
                for k, j in enumerate(PARTS["hgrn_in"]):
                    run_job(l, START["hgrn_in"] + k, j)
                    if j.kind == "ada" and j.arg in (9, 10):
                        forget(l, j.arg - 9)
                    if j.kind == "fm" and j.arg[:2] == ("hq", HQ):
                        for d in range(2):
                            dve.wait_ge(ln_out.sem, ln_out.at(l, d + 1))
                            v = lf[:, :, d * BW:(d + 1) * BW]
                            dve.tensor_tensor(v, v, lnb[:, d, :, :], ALU.add).then_inc(*own.tell(f_ready, f_ready.at(l, d + 1)))
                dve.wait_ge(params_loaded.sem, params_loaded.at(l, 32))
                v = nab.rearrange("p e (r c) -> p (e r) c", c=HD)
                dve.tensor_tensor(v, v, c("nam").unsqueeze(1).to_broadcast([P, HEADS * 14, HD]), ALU.add).then_inc(*own.step())
                hgrn(l)
                hgrn_norm(l)
                for k, j in enumerate(PARTS["mix_in"]):
                    run_job(l, START["mix_in"] + k, j)
                    if j.kind == "ada" and j.arg == 16:
                        mlp_norm(l)
                attention(l)
                dve.wait_ge(kv_out.sem, kv_out.at(l, 5 * 16))
                for part in ("merge", "out"):
                    for k, j in enumerate(PARTS[part]):
                        run_job(l, START[part] + k, j)
                norm_x(l, 1)
                router(l)
                with dve.Fori(0, GROUPS) as g:
                    own.group(g)
                    dve.tensor_copy(cg[:, :, :], comb[:, :, g, :]).then_inc(*own.tell(cg_ready, cg_ready.at(l, g + 1)))
                    for k, j in enumerate(PARTS["moe"]):
                        run_job(l, START["moe"] + k, j, g)
                    own.end_group()
                own.end_layer()
            own.layer(DEPTH)
            norm_x(DEPTH, 0)

        @block.gpsimd
        def _(pool):
            with pool.Fori(0, DEPTH) as l:
                for u, (d, stream, i) in enumerate(HGRN_UNITS):
                    v = u % 2
                    pool.wait_ge(kT_ready.sem, kT_ready.at(l, u + 1))
                    for a in range(2):
                        pool.wait_ge(ex_ready.sem, ex_ready.at(l, 2 * u + a + 1))
                        pool.tensor_tensor(ke[v][:, a, :, :], ex[v][:, a, 0:LEVELS, :],
                                           kT[v][:, a, :].unsqueeze(1).to_broadcast([P, LEVELS, P]), ALU.mult)\
                            .then_inc(ke_ready.sem, 1)
                    pool.wait_ge(es_ready.sem, es_ready.at(l, u + 1))
                    if u >= 2:
                        pool.wait_ge(o_full.sem, o_full.at(l, u - 1))
                    pool.tensor_tensor(kd[v], kk[:, i, d * BW:(d + 1) * BW], es[v], ALU.mult).then_inc(kd_ready.sem, 1)
                for u, (b, hd, i) in enumerate(ATT_UNITS):
                    n = n_keys(b, i)
                    pool.wait_ge(att_rinv.sem, att_rinv.at(l, u + 1))
                    alone(pool)
                    pool.tensor_scalar(sbs[:, u % 3, 0:n], sbs[:, u % 3, 0:n], rinv[:, u % 3:u % 3 + 1], None,
                                       ALU.mult).then_inc(att_p.sem, 1)
                with pool.Fori(0, GROUPS) as g:
                    for e in range(EPG):
                        pool.wait_ge(*out_of(l, moe_at("cb", e), g))
                        for ft in range(2):
                            pool.wait_ge(*out_of(l, moe_at("mup", (e, ft)), g))
                            v = act_t[:, 2 * e + ft, :]
                            pool.tensor_tensor(v, v, cb[:, e, :], ALU.mult).then_inc(act_ready.sem, 1)


def constants():
    r = np.arange(P)
    cst = {}
    cst["ident"] = np.eye(P)
    cst["ones"] = np.ones((P, P))
    cst["block"] = (r[:, None] // HD == r[None, :] // HD) * 1.0
    perm = np.zeros((P, P))
    for m in range(P):
        if m % 32 < 16:
            perm[m + 16, m] = -1.0
        else:
            perm[m - 16, m] = 1.0
    cst["perm"] = perm
    decay = np.zeros((P, 2, 8, P))
    mask = np.zeros((P, 2, LEVELS, HD), np.float32)
    rr, t = r[:, None], r[None, :]
    for lev in range(LEVELS):
        half = HD >> lev
        mid = t // (2 * half) * (2 * half) + half
        second = t >= mid
        decay[:, 0, lev] = np.where(second, (rr >= mid) & (rr <= t), (rr > t) & (rr < mid))
        decay[:, 1, lev] = np.where(second, (rr >= mid) & (rr < t), (rr >= t) & (rr < mid))
        block = r // (2 * half)
        in_second = r % (2 * half) >= half
        for d in range(2):
            queries = np.nonzero(in_second == (d == 0))[0]
            mask[:, d, lev] = (block[:, None] == block[queries][None, :]) & (in_second[:, None] == (d == 1))
    decay[:, 0, 7] = rr <= t
    decay[:, 1, 7] = rr >= t
    cst["decay"] = decay.reshape(P, -1)
    tail = np.zeros((P, 2, P))
    tail[:, 0] = rr > t
    tail[:, 1] = rr < t
    cst["tail"] = tail.reshape(P, -1)
    f = np.float32
    inv = (f(1.0) / (f(10000.0) ** (np.arange(0, 32, 2, dtype=f) / f(32)))).astype(f)
    tok = np.arange(LAT)
    ang = np.zeros((HD, LAT), f)
    for m in range(HD):
        pos = (tok // 64 if m < 32 else tok % 64).astype(f)
        ang[m] = pos * inv[m % 16]
    cst["cos"] = np.tile(np.cos(ang), (2, 1))
    cst["sin"] = np.tile(np.sin(ang), (2, 1))
    swm = np.zeros((P, 3, P))
    swm[:, 0] = np.where(t >= rr, 0, NEG)
    swm[:, 2] = np.where(t <= rr, 0, NEG)
    cst["swm"] = swm.reshape(P, -1)
    col = r % 64
    start = np.clip(col - 8, 0, 48)[:, None]
    c2 = np.arange(64)[None, :]
    cst["nam"] = np.where((c2 >= start) & (c2 < start + 16), 0, NEG)
    flat = np.concatenate([cst[name].astype(f) for name in CST], axis=1)
    assert flat.shape[1] == N_CST
    return np.ascontiguousarray(flat), mask.reshape(P, 2 * LEVELS, HD)


def fmaj(a):
    return np.asarray(a).reshape(-1, P, a.shape[-1]).transpose(1, 0, 2)


def lay_out(inp):
    inp = {k: np.asarray(v) for k, v in inp.items()}
    f = np.float32
    cst, mask = constants()
    arrays = {"cst": cst, "msk": mask}
    arrays["xT"] = fmaj(np.concatenate([inp["x_sample"][0], inp["x_prompt"][0]], 0).T)
    arrays["cT"] = fmaj(np.stack([inp["c"][0], inp["c_ctx"]], 1))
    arrays["fg"] = inp["final_g"].reshape(KT, P).T
    arrays["lbr"] = np.broadcast_to(inp["hgrn_lb"].reshape(1, DEPTH, 2 * BW), (P, DEPTH, 2 * BW))
    sw = np.concatenate([np.arange(hh * HD, (hh + 1) * HD) for hh in (0, 2, 1, 3)])
    ws = np.empty((DEPTH * PAIRS, P, 2, UNIT), f)
    lpa = np.empty((DEPTH, P, N_LPA), f)
    lpb = np.empty((P, DEPTH, N_LPB), f)
    for l in range(DEPTH):
        w_in = inp["w_in"][l].copy()
        w_in[:, COL["sq"]:COL["sq"] + BW] = w_in[:, COL["sq"] + sw]
        w_branch = inp["w_branch"][l].copy()
        w_branch[3] = w_branch[3][sw]

        def cols(w, c0, n=P):
            return w[:, c0:c0 + n].reshape(-1, P, n).transpose(1, 0, 2)

        def put(u, spec, g=0):
            dst = ws[l * PAIRS + u // 2, :, u % 2]
            kind = spec[0]
            if kind == "ada":
                v = cols(inp["w_ada"][l], spec[1] * P)
            elif kind == "in":
                v = cols(w_in, spec[1])
            elif kind == "tm":
                v = cols(w_in, spec[1], 256).reshape(P, 2, UNIT)[:, spec[2]]
            elif kind == "branch":
                v = cols(w_branch.reshape(NB * BW, D), spec[1] * P)
            elif kind == "out":
                v = cols(inp["w_out"][l], spec[1] * P)
            elif kind in ("moe_gate", "moe_up"):
                w = inp["moe_w_gate" if kind == "moe_gate" else "moe_w_up"][l, g * EPG + spec[1]]
                v = cols(w, spec[2] * P)
            elif kind == "moe_down":
                w = inp["moe_w_down"][l, g * EPG:(g + 1) * EPG].reshape(EPG * FF, D)
                v = cols(w, spec[1] * P)
            dst[...] = v.reshape(P, UNIT)

        for u, spec in enumerate(UNITS0):
            put(u, spec)
        for g in range(GROUPS):
            for u, spec in enumerate(UNITS_G):
                put(len(UNITS0) + g * len(UNITS_G) + u, spec, g)

        parts = {}
        q = np.arange(P)
        e = np.arange(14)
        dr = e[None, :] + 1 - (q[:, None] >= 64)
        dc = np.clip(np.arange(64)[None, :] - (q[:, None] % 64), -15, 15) + 15
        rpb = inp["na_rpb"][l]
        parts["nab"] = rpb[:, dr[:, :, None], dc[:, None, :]].transpose(1, 0, 2, 3)
        parts["nk"] = fmaj(inp["cache_na_k"][0, l].reshape(P, BW).T)
        parts["nv"] = inp["cache_na_v"][0, l].reshape(P, BW)
        parts["sk"] = inp["cache_swa_k"][0, l].reshape(P, P).T
        parts["sv"] = inp["cache_swa_v"][0, l].reshape(P, P)
        parts["ws"] = inp["smlp_ws"][l].transpose(2, 0, 1)
        parts["smb"] = np.repeat(inp["smlp_b"][l].reshape(2, 2, 1, P), HD, 2).reshape(2, P, P).transpose(1, 0, 2)
        parts["sink"] = np.broadcast_to(inp["swa_sink"][l][None], (P, HEADS))
        lpa[l] = np.concatenate([parts[k].reshape(P, -1) for k in LPA], 1)
        parts["b_ada"] = inp["b_ada"][l].reshape(48, P).T
        parts["n1"] = inp["norm1_g"][l].reshape(KT, P).T
        parts["n2"] = inp["norm2_g"][l].reshape(KT, P).T
        parts["on"] = inp["hgrn_onorm_g"][l].reshape(2, P).T
        parts["wr"] = fmaj(np.concatenate([inp["router_g_w"][l], inp["router_e_w"][l]], 1))
        parts["rb"] = np.broadcast_to(np.concatenate([inp["router_g_b"][l], inp["router_e_b"][l]])[None], (P, 20))
        lpb[:, l] = np.concatenate([parts[k].reshape(P, -1) for k in LPB], 1)
    arrays["ws"] = ws.reshape(DEPTH * PAIRS, P, 2 * UNIT)
    arrays["lpa"] = lpa
    arrays["lpb"] = lpb
    s = inp["state_hgrn"][0].reshape(DEPTH, 2, 2, 2, HD, HD)
    arrays["st_in"] = s.transpose(0, 3, 4, 1, 2, 5).reshape(DEPTH, P, 2, 2, HD)
    return {k: np.ascontiguousarray(v) for k, v in arrays.items()}


OUTS = {
    "y": (P, KT, T), "nk_out": (DEPTH, P, 2, P), "nv_out": (DEPTH, P, BW), "sk_out": (DEPTH, P, P),
    "sv_out": (DEPTH, P, P), "st_out": (DEPTH, P, 2, 2, HD),
}


def make(nc, arrays):
    A = {k: nc.dram_tensor(k, v.shape, mybir.dt.from_np(v.dtype), kind="ExternalInput").ap() for k, v in arrays.items()}
    for k, shape in OUTS.items():
        A[k] = nc.dram_tensor(k, shape, F32, kind="ExternalOutput").ap()
    build(nc, A)
    return nc


def unpack(r):
    y = r["y"].transpose(2, 1, 0).reshape(T, D)
    nk = r["nk_out"].transpose(0, 3, 2, 1).reshape(1, DEPTH, CTX, HEADS, HD)
    nv = r["nv_out"].reshape(1, DEPTH, CTX, HEADS, HD)
    sk = r["sk_out"].transpose(0, 2, 1).reshape(1, DEPTH, CTX, 2, HD)
    sv = r["sv_out"].reshape(1, DEPTH, CTX, 2, HD)
    s = r["st_out"].reshape(DEPTH, 2, HD, 2, 2, HD).transpose(0, 3, 4, 1, 2, 5).reshape(1, DEPTH, 2, HEADS, HD, HD)
    out = (y[LAT:][None], y[:LAT][None], nk, nv, sk, sv, s)
    return tuple(np.ascontiguousarray(v) for v in out)


def kernel(**inputs):
    import concourse.bacc as bacc
    from concourse.bass_utils import run_bass_kernel_spmd

    arrays = lay_out(inputs)
    nc = bacc.Bacc("TRN2", target_bir_lowering=False, num_devices=1)
    make(nc, arrays)
    r = run_bass_kernel_spmd(nc, [arrays], core_ids=[0])
    return unpack(r.results[0])
```

```python
from contextlib import ExitStack

import numpy as np

import concourse.bass as bass
from concourse import mybir

F32 = mybir.dt.float32
U8 = mybir.dt.uint8
ALU = mybir.AluOpType
ACT = mybir.ActivationFunctionType
AX = mybir.AxisListType

P = 128
D = 1024
DEPTH = 2
CTX = 128
LAT = 512
T = LAT + CTX
KT = D // P
TILES = T // P
LT = LAT // P
CT = LT
BW = 256
HD = 64
HEADS = BW // HD
NB = 4
GROUPS = 4
EPG = 4
FF = 256
NBLK = (T - GROUPS) // P + GROUPS
EPS = 1e-6
LN_SPLIT = 2.0 ** 50
TINY = 1e-30
FILL_LEVELS = [(0, 1, 2), (3, 4, 5), (6, 7)]
FILLS = len(FILL_LEVELS)
LEVELS = 7
NEG = -1e30
ADA_BEFORE_STATS = 5

UNIT = KT * P
RING = 4

HQ, HOG, NAQ, NAK, MU, SQ, SK = 0, 2, 4, 6, 8, 10, 12
N_FM = 13
BRANCH_AT = [HQ, NAQ, MU, SQ]

COL = dict(hq=0, hi=256, hff=512, hfb=768, hog=1024, naq=1280, nak=1536, nav=1792, mu=2048, mv=2304,
           sq=2560, sk=2816, sv=2944, gates=3072)

HGRN_UNITS = [(0, 0, CT)] + [(0, 1, i) for i in range(LT)] + [(1, 0, CT)] + [(1, 1, i) for i in reversed(range(LT))]
ATT_UNITS = [(b, h, i) for b in ("na", "swa") for h in range(HEADS) for i in range(TILES)]


class Job:
    def __init__(self, kind, arg, units=()):
        self.kind, self.arg, self.units = kind, arg, tuple(units)


def make_plan():
    units, parts = [], {}

    def take(*specs):
        at = len(units)
        units.extend(specs)
        return list(range(at, at + len(specs)))

    def ada(i):
        return [Job("ada", i, take(("ada", 2 * i), ("ada", 2 * i + 1)))]

    def fm(name, dst):
        u = take(("in", COL[name]), ("in", COL[name] + P))
        return [Job("fm", (name, dst + a, 0), [u[a]]) for a in range(2)]

    def tm(name):
        u = take(("tm", COL[name], 0), ("tm", COL[name], 1))
        return [Job("tm", (name, 0, LT, 256), u), Job("tm", (name, LT, TILES, 256), u)]

    parts["ada"] = sum([ada(i) for i in range(8)], [])
    parts["hgrn_in"] = (tm("hff") + ada(8) + tm("hfb") + ada(9) + tm("hi") + ada(10) + fm("hq", HQ) + ada(11)
                        + fm("hog", HOG) + ada(12))
    parts["hgrn_out"] = [Job("onorm", a) for a in range(2)]
    mix = fm("nak", NAK) + ada(13) + fm("naq", NAQ) + ada(14) + tm("nav") + ada(15) + tm("mv") + ada(16)
    u = take(("in", COL["sk"]), ("in", COL["sv"]))
    mix += [Job("fm", ("sk", SK, 0), [u[0]]), Job("tm", ("sv", 0, LT, P), [u[1]]), Job("tm", ("sv", LT, TILES, P), [u[1]])]
    mix += ada(17) + fm("sq", SQ) + ada(18) + fm("mu", MU) + ada(19)
    mix += [Job("rope", t) for t in (SK, SQ, SQ + 1)] + [Job("mlp", a) for a in range(2)]
    parts["mix_in"] = mix
    merge = []
    for dp in range(KT // 2):
        for d in (2 * dp, 2 * dp + 1):
            u = take(("branch", d), *[("in", COL["gates"] + n * D + d * P) for n in range(NB)])
            for n in range(NB):
                merge += [Job("gate", (d, n), [u[1 + n]]), Job("proj", (d, n), [u[0]])]
    parts["merge"] = merge
    out = []
    for d in range(0, KT, 2):
        u = take(("out", d), ("out", d + 1))
        out += [Job("out", d + a, [u[a]]) for a in range(2)] + ada(20 + d // 2)
    parts["out"] = out
    before = len(units)
    parts["sort"] = [Job("rows", i) for i in range(TILES)] + [Job(kind, 0) for kind in
                                                              ("rank", "total", "place", "gather", "weights")]
    moe = []

    def expert(kind, e):
        u = take((kind, e, 0), (kind, e, 1))
        return [Job(kind, e, u)]

    for e in range(EPG):
        moe += expert("moe_gate", e)
        if e >= 1:
            moe += expert("moe_down", e - 1)
        moe += expert("moe_up", e)
    parts["moe"] = moe + [Job("gather", 0)] + expert("moe_down", EPG - 1) + [Job("weights", 0)]
    parts["moe_last"] = [j for j in parts["moe"] if j.kind not in ("gather", "weights")]
    group_units = units[before:]
    parts["back"] = [Job("back", d) for d in range(KT)]
    jobs = [j for name, p in parts.items() if name not in ("moe_last", "back") for j in p]
    read_by = {}
    for n, j in enumerate(jobs):
        for x in j.units:
            read_by[x // 2] = n + 1
    start, n = {}, 0
    for name, p in parts.items():
        if name == "moe_last":
            n += (NBLK - 2) * len(parts["moe"])
        start[name] = n
        n += len(p)
    return units[:before], group_units, parts, start, read_by


UNITS0, UNITS_G, PARTS, START, READ_BY = make_plan()
PAIRS0 = len(UNITS0) // 2
PAIRS_G = len(UNITS_G) // 2
PAIRS = PAIRS0 + NBLK * PAIRS_G
DRAM_PAIRS = PAIRS0 + GROUPS * PAIRS_G
JOBS_G = len(PARTS["moe"])
JOBS = START["back"] + KT
assert START["moe"] % 2 == 0 and JOBS_G % 2 == 0 and JOBS % 2 == 0 and PAIRS0 % RING == 0 and PAIRS_G % RING == 0


N_DVE_ADA = sum(j.kind == "ada" for part in ("mix_in", "out") for j in PARTS[part])
FIRST_DVE_ADA = 24 - N_DVE_ADA


def read_by(pair):
    return READ_BY[pair]


def job_at(part, kind, arg):
    for n, j in enumerate(PARTS[part]):
        if j.kind == kind and (j.arg == arg or (kind in ("fm", "tm") and j.arg[:2] == arg)):
            return START[part] + n
    raise KeyError((part, kind, arg))


LPA, n = {}, 0
for name, w in (("nab", HEADS * 14 * HD), ("nk", 2 * P), ("nv", BW), ("sk", P), ("sv", P), ("ws", 4 * P),
                ("smb", 2 * P), ("sink", HEADS)):
    LPA[name] = (n, n + w)
    n += w
N_LPA = n
LPB, n = {}, 0
for name, w in (("b_ada", 48), ("n1", KT), ("n2", KT), ("on", 2), ("wr", KT * 20), ("rb", 20)):
    LPB[name] = (n, n + w)
    n += w
N_LPB = n
CST, n = {}, 0
for name, w in (("ident", P), ("ones", P), ("block", P), ("perm", P), ("decay", 2 * 8 * P), ("tail", 2 * P),
                ("cos", LAT), ("sin", LAT), ("swm", 3 * P), ("nam", HD), ("iota", P), ("slotid", NBLK), ("blockid", NBLK)):
    CST[name] = (n, n + w)
    n += w
N_CST = n


def key_range(b, i):
    if i == CT:
        return LAT, T
    if b == "na":
        return 0, LAT
    return max(0, i - 1) * P, min(LT, i + 2) * P


def n_keys(b, i):
    lo, hi_ = key_range(b, i)
    return hi_ - lo + (P if i < LT else 0)


class Counted:

    def __init__(self, sem, per_layer, start):
        self.sem, self.per, self.start = sem, per_layer, start

    def at(self, layer, n):
        return layer * self.per + (n + self.start)


class Own:

    def __init__(self, eng, sem, per_layer, per_group=0):
        self.eng, self.sem, self.per, self.per_group = eng, sem, per_layer, per_group
        self.base, self.n, self.last = 0, 0, None

    def layer(self, l):
        self.base, self.n, self.last = l * self.per, 0, None

    def group(self, g):
        self.first = self.n
        self.outer = self.base
        self.base = self.base + g * self.per_group
        self.last = None

    def end_group(self):
        assert self.n - self.first == self.per_group, ("per group", self.n - self.first)
        self.n = self.first + (NBLK - 1) * self.per_group
        self.base, self.last = self.outer, None

    def end_layer(self):
        assert self.n == self.per, ("per layer", self.n)

    def step(self):
        self.n += 1
        self.last = self.sem, self.base + self.n
        return self.sem, 1

    def tell(self, sig, value):
        self.last = sig.sem, value
        return sig.sem, 1


OWN_STEPS = {"act": (7, 0), "dve": (493, 1)}


def build(nc, A):
    ctx = ExitStack()
    with ctx:
        def sb(name, shape, dt=F32):
            return ctx.enter_context(nc.sbuf_tensor(name + "_sb", shape, dt))

        def sem(name):
            return ctx.enter_context(nc.semaphore(name))

        def counted(name, per_layer, start=0):
            return Counted(sem(name), per_layer, start)

        ring = sb("ring", [P, RING, 2 * UNIT])
        x = sb("x", [P, KT, T])
        h = sb("h", [P, KT, T])
        fm = sb("fm", [P, N_FM, T])
        tmr = sb("tmr", [P, 6400])
        scr = sb("scr", [P, 5120])
        o = sb("o", [P, 2, T])
        lpa = sb("lpa", [P, N_LPA])
        lpb = sb("lpb", [P, DEPTH, N_LPB])
        lpc = sb("lpc", [P, N_LPB])
        cst = sb("cst", [P, N_CST])
        msk = sb("msk", [P, 2, LEVELS, HD], U8)
        lbs = sb("lbs", [P, DEPTH, 2 * BW])
        omlb = sb("omlb", [P, 2 * BW])
        st = sb("st", [P, 2, 2, 2, HD])
        mod = sb("mod", [P, 48, 2])
        amul = sb("amul", [P, 2, KT, 2])
        cond = sb("cond", [P, KT, 2])
        cneg = sb("cneg", [P, KT, 2])
        fg = sb("fg", [P, KT])
        eps = sb("eps", [P, 1])
        tot = sb("tot", [P, 2, 2])
        nmx = sb("nmx", [P, 3])
        sums = sb("sums", [P, 3])
        rinv = sb("rinv", [P, 3])
        vstat = sb("vstat", [P, 20])
        lt = sb("lt", [P, TILES, 20])
        rt = sb("rt", [P, 14, TILES, 4])
        rank = sb("rank", [P, TILES, GROUPS])
        n_blocks = sb("n_blocks", [P, GROUPS])
        end_block = sb("end_block", [P, GROUPS])
        first_slot = sb("first_slot", [P, GROUPS])
        place = sb("place", [P, TILES, 1])
        ahead = sb("ahead", [P, TILES, 1])
        group_of = sb("group_of", [P, 2, NBLK])
        table = sb("table", [P, NBLK], mybir.dt.int32)
        cs = sb("cs", [P, EPG])
        ps = ctx.enter_context(nc.psum_tensor("ps", [P, 8, 512], F32))

        def view(tensor, at, *shape):
            n = int(np.prod(shape))
            v = tensor[:, at:at + n]
            if len(shape) == 2:
                v = v.rearrange("p (a b) -> p a b", a=shape[0])
            if len(shape) == 3:
                v = v.rearrange("p (a b c) -> p a b c", a=shape[0], b=shape[1])
            return v

        lf = view(tmr, 0, TILES, 2 * BW)
        kk = view(tmr, 2560, TILES, 2 * BW)
        hi = view(tmr, 5120, TILES, BW)
        nav = view(tmr, 0, TILES, BW)
        mv = view(tmr, 1280, TILES, BW)
        sv = view(tmr, 2560, TILES, P)
        merged = view(tmr, 0, KT, T)
        h_rows = view(tmr, 0, TILES, D)
        TM_DST = dict(hff=kk[:, :, 0:BW], hfb=kk[:, :, BW:2 * BW], hi=hi, nav=nav, mv=mv, sv=sv)
        lnb = view(scr, 0, 2, TILES, BW)
        osq = view(scr, 0, 2, T)
        ors = view(scr, 1280, 2, T)
        sbs = view(scr, 0, 3, T + 1)
        pts = view(scr, 1923, 2, T)
        mvsq = view(scr, 3203, TILES, BW)
        sg = view(scr, 0, 2, T)
        mt = view(scr, 1280, 2, T)
        sel = view(scr, 0, TILES, P)
        hb = view(scr, 640, KT, P)
        ab = view(scr, 1664, 2, 2, P)
        sgb = view(scr, 2176, 2, 2 * P)
        place_row = view(scr, 2688, T)
        nsq = view(scr, 0, 2, T)
        rs = view(scr, 1280, T)
        xn = view(scr, 1920, 2, T)
        lbraw = view(scr, 0, DEPTH, 2 * BW)
        mraw = view(scr, 4096, 2 * LEVELS, HD)

        ada_sums = o[:, :, 0:2 * P]
        fm_rows = fm[:, :, :].rearrange("p n t -> p (n t)")
        hgrn_scratch = [(scr, 0), (fm_rows, NAQ * T)]
        ex = [view(t, at, 2, 8, P) for t, at in hgrn_scratch]
        ke = [view(t, at + 2048, 2, LEVELS, P) for t, at in hgrn_scratch]
        kT = [view(t, at + 3840, 2, P) for t, at in hgrn_scratch]
        es = [view(t, at + 4096, BW) for t, at in hgrn_scratch]
        kd = [view(t, at + 4352, BW) for t, at in hgrn_scratch]
        at_ = [view(t, at + 4608, HEADS, P) for t, at in hgrn_scratch]

        y_blocks = view(fm_rows, 0, NBLK, D)
        unsort = view(h[:, :, :].rearrange("p k t -> p (k t)"), 0, NBLK, T)

        def c(name, *shape):
            a, b = CST[name]
            return view(cst, a, *(shape or (b - a,)))

        def pa(name, *shape):
            a, b = LPA[name]
            return view(lpa, a, *(shape or (b - a,)))

        def pb(name, *shape):
            a, b = LPB[name]
            return view(lpc, a, *(shape or (b - a,)))

        nab = pa("nab", HEADS, 14 * HD)

        def slot(n):
            return ps[:, 2 * (n % 2):2 * (n % 2) + 2, :].rearrange("p b c -> p (b c)")

        def banks(b, n):
            return ps[:, b:b + n, :].rearrange("p b c -> p (b c)")

        loaded = sem("loaded")
        n_loads = 4
        c_loaded = sem("c_loaded")
        x_loaded = sem("x_loaded")
        params_loaded = counted("params_loaded", 32)
        arrived = [counted(f"arrived{s}", 16 * PAIRS // RING) for s in range(RING)]
        job_full = counted("job_full", JOBS)
        job_out = [counted(f"job_out{s}", JOBS // 2, 1) for s in range(2)]
        kv_out = counted("kv_out", 5 * 16)
        y_out = sem("y_out")
        lb_diff = sem("lb_diff")
        start_exp = sem("start_exp")
        cond_ready = sem("cond_ready")
        small_ready = counted("small_ready", 1)
        mod_full = counted("mod_full", 2)
        sums_ready = counted("sums_ready", N_DVE_ADA)
        sq_ready = counted("sq_ready", 2 * KT)
        sq_used = counted("sq_used", 2 * KT)
        rs_ready = counted("rs_ready", 2)
        xn_ready = counted("xn_ready", 2 * KT)
        h_ready = counted("h_ready", 2 * KT)
        ln_in = counted("ln_in", 2)
        ln_out = counted("ln_out", 2)
        f_ready = counted("f_ready", 2)
        neg_exp = counted("neg_exp", 4)
        NU = len(HGRN_UNITS)
        decay_full = counted("decay_full", 2 * NU)
        tail_full = counted("tail_full", NU)
        ex_ready = counted("ex_ready", 2 * NU)
        es_ready = counted("es_ready", NU)
        kT_ready = counted("kT_ready", NU)
        ke_ready = counted("ke_ready", 2 * NU)
        kd_ready = counted("kd_ready", NU)
        qe_ready = counted("qe_ready", 2 * NU)
        score_full = counted("score_full", FILLS * NU)
        score_out = counted("score_out", FILLS * NU)
        o_full = counted("o_full", NU)
        s_ready = counted("s_ready", NU)
        osq_ready = counted("osq_ready", 2)
        a_done = counted("a_done", 2)
        v_stat = counted("v_stat", 1)
        v_rs = counted("v_rs", 1)
        v_ready = counted("v_ready", 1)
        NAT = len(ATT_UNITS)
        att_s_full = counted("att_s_full", NAT)
        att_s_out = counted("att_s_out", NAT)
        att_exp = counted("att_exp", NAT)
        att_rinv = counted("att_rinv", NAT)
        att_p = counted("att_p", NAT)
        att_t_full = counted("att_t_full", NAT)
        att_t_out = counted("att_t_out", NAT)
        att_o_full = counted("att_o_full", NAT)
        att_o_out = counted("att_o_out", NAT)
        m_ready = counted("m_ready", KT)
        router_full = counted("router_full", 1)
        r_in = counted("r_in", 2)
        r_exp = counted("r_exp", 2)
        group_ready = counted("group_ready", 1)
        place_ready = counted("place_ready", 1)
        table_ready = counted("table_ready", 1)
        sel_ready = counted("sel_ready", NBLK)
        weight_ready = counted("weight_ready", 1)
        unsort_ready = counted("unsort_ready", 1)
        start_steps = sem("start_steps")
        passed = sem("passed")
        own_sem = {e: sem(f"{e}_steps") for e in OWN_STEPS}

        block = ctx.enter_context(nc.Block())

        def out_at(l, n, g=None):
            value = job_out[n % 2].at(l, n // 2 + 1)
            return job_out[n % 2], value if g is None else value + g * (JOBS_G // 2)

        def out_of(l, n, g=None):
            sig, value = out_at(l, n, g)
            return sig.sem, value

        def full(l, n, g=None):
            return job_full.sem, job_full.at(l, n + 1 if g is None else n + 1 + g * JOBS_G)

        def alone(eng):
            eng.sem_inc(passed)

        def moe_at(kind, arg):
            return START["moe"] + [k for k, j in enumerate(PARTS["moe"]) if j.kind == kind and j.arg == arg][0]

        @block.sync
        def _(sp):
            def load(l, pair, at=None):
                n = l * DRAM_PAIRS + (pair if at is None else at)
                sp.dma_start(ring[:, pair % RING, :], A["ws"][n]).then_inc(arrived[pair % RING].sem, 16)

            def group_pairs(block):
                group = nc.values_load(table[0:1, bass.ds(block, 1)], engines=[mybir.EngineType.SP], min_val=0,
                                       max_val=GROUPS - 1,
                                       skip_runtime_bounds_check_because="a sum of GROUPS - 1 comparisons' results")
                return PAIRS0 + group * PAIRS_G

            def layer(l):
                for pair in range(RING, PAIRS0):
                    sp.wait_ge(job_full.sem, job_full.at(l, read_by(pair - RING)))
                    load(l, pair)
                for pair in range(PAIRS0, PAIRS0 + RING):
                    sp.wait_ge(job_full.sem, job_full.at(l, read_by(pair - RING)))
                    load(l, pair)
                sp.wait_ge(table_ready.sem, table_ready.at(l, 1))
                alone(sp)
                with sp.Fori(0, NBLK - 1) as g:
                    first = group_pairs(g)
                    for k in range(RING, PAIRS_G):
                        sp.wait_ge(job_full.sem, job_full.at(l, read_by(PAIRS0 + k - RING) + g * JOBS_G))
                        load(l, PAIRS0 + k, first + k)
                    first = group_pairs(g + 1)
                    for k in range(RING):
                        sp.wait_ge(job_full.sem, job_full.at(l, read_by(PAIRS0 + PAIRS_G + k - RING) + g * JOBS_G))
                        load(l, PAIRS0 + k, first + k)
                first = group_pairs(NBLK - 1)
                for k in range(RING, PAIRS_G):
                    sp.wait_ge(job_full.sem, job_full.at(l, read_by(PAIRS0 + k - RING) + (NBLK - 1) * JOBS_G))
                    load(l, PAIRS0 + k, first + k)

            for pair in range(RING):
                load(0, pair)
            with sp.Fori(0, DEPTH - 1) as l:
                layer(l)
                for pair in range(RING):
                    sp.wait_ge(job_full.sem, job_full.at(l, read_by(PAIRS0 + PAIRS_G + pair - RING) + (NBLK - 1) * JOBS_G))
                    load(l + 1, pair)
            layer(DEPTH - 1)
            sp.wait_ge(h_ready.sem, h_ready.at(DEPTH, KT))
            sp.dma_start(A["y"], h[:, :, :]).then_inc(y_out, 16)
            sp.wait_ge(y_out, 16)

        @block.tensor
        def _(pe):
            def unit(x_):
                pair = x_ // 2
                return view(ring[:, pair % RING, :], (x_ % 2) * UNIT, KT, P)

            def stats(l, k):
                for kt in range(KT):
                    pe.wait_ge(sq_ready.sem, sq_ready.at(l, k * KT + kt + 1))
                    for b, lo, hi_ in ((4, 0, LAT), (5, LAT, T)):
                        mm = pe.matmul(ps[:, b, 0:hi_ - lo], c("ones"), nsq[:, kt % 2, lo:hi_],
                                       start=(kt == 0), stop=(kt == KT - 1))
                    mm.then_inc(sq_used.sem, 1)

            def product(dst, w, src, n_k):
                for k in range(n_k):
                    for lo, hi_ in ((0, LAT), (LAT, T)):
                        mm = pe.matmul(dst[:, lo:hi_], w(k), src(k, lo, hi_), start=(k == 0), stop=(k == n_k - 1))
                return mm

            arrived_pairs = set()

            def run_job(l, n, j, g=None):
                count = n // 2 if g is None else n // 2 + g * (JOBS_G // 2)
                pe.wait_ge(job_out[n % 2].sem, job_out[n % 2].at(l, count))
                summed = j.kind == "ada" and j.arg >= FIRST_DVE_ADA
                if summed:
                    pe.wait_ge(sums_ready.sem, sums_ready.at(l, j.arg - FIRST_DVE_ADA + 1))
                for u in j.units:
                    if u // 2 not in arrived_pairs and not summed:
                        pair = u // 2
                        value = 16 * (pair // RING + 1)
                        if g is not None:
                            value = value + g * (16 * PAIRS_G // RING)
                        pe.wait_ge(arrived[pair % RING].sem, arrived[pair % RING].at(l, value))
                        arrived_pairs.add(pair)
                dst = slot(n)
                if summed:
                    for a in range(2):
                        for w in range(2):
                            mm = pe.matmul(dst[:, 2 * a + w:2 * a + w + 1], ada_sums[:, w, a * P:(a + 1) * P],
                                           c("ones")[:, 0:1], start=True, stop=True)
                elif j.kind == "ada":
                    for a in range(2):
                        w = unit(j.units[a])
                        for k in range(KT):
                            mm = pe.matmul(dst[:, 2 * a:2 * a + 2], w[:, k, :], cond[:, k, :], start=(k == 0),
                                           stop=(k == KT - 1))
                elif j.kind in ("fm", "gate", "mgate", "mup"):
                    w = unit(j.units[0])
                    mm = product(dst, lambda k: w[:, k, :], lambda k, a, b: h[:, k, a:b], KT)
                elif j.kind == "tm":
                    _, i0, i1, wide = j.arg
                    if wide == P:
                        w = unit(j.units[0])
                    else:
                        w = view(ring[:, (j.units[0] // 2) % RING, :], 0, KT, wide)
                    for i in range(i0, i1):
                        for k in range(KT):
                            mm = pe.matmul(dst[:, (i - i0) * wide:(i - i0 + 1) * wide], h[:, k, i * P:(i + 1) * P],
                                           w[:, k, :], start=(k == 0), stop=(k == KT - 1))
                elif j.kind == "onorm":
                    pe.wait_ge(osq_ready.sem, osq_ready.at(l, j.arg + 1))
                    mm = product(dst, lambda k: c("block"), lambda k, a, b: osq[:, j.arg, a:b], 1)
                elif j.kind == "rope":
                    a = j.arg
                    name = ("sk", SK) if a == SK else ("sq", a)
                    if (job_at("mix_in", "fm", name) - n) % 2:
                        pe.wait_ge(*out_of(l, job_at("mix_in", "fm", name)))
                    mm = pe.matmul(dst[:, 0:LAT], c("perm"), fm[:, a, 0:LAT], start=True, stop=True)
                elif j.kind == "mlp":
                    pe.wait_ge(v_ready.sem, v_ready.at(l, 1))
                    for gg in (2 * j.arg, 2 * j.arg + 1):
                        at = HD * (gg % 2)
                        for i in range(TILES):
                            mm = pe.matmul(dst[at:at + HD, i * P:(i + 1) * P], mv[:, i, gg * HD:(gg + 1) * HD],
                                           pa("ws", 4, P)[:, gg, :], start=True, stop=True)
                elif j.kind == "proj":
                    d, nb_ = j.arg
                    if j.arg == (0, 0):
                        pe.wait_ge(a_done.sem, a_done.at(l, 2))
                        pe.wait_ge(att_o_out.sem, att_o_out.at(l, NAT))
                    w = view(ring[:, (j.units[0] // 2) % RING, :], (j.units[0] % 2) * UNIT, NB * 2, P)
                    mm = product(dst, lambda k: w[:, 2 * nb_ + k, :],
                                 lambda k, a, b: fm[:, BRANCH_AT[nb_] + k, a:b], 2)
                elif j.kind == "out":
                    if j.arg == 0:
                        pe.wait_ge(m_ready.sem, m_ready.at(l, KT))
                    w = unit(j.units[0])
                    mm = product(dst, lambda k: w[:, k, :], lambda k, a, b: merged[:, k, a:b], KT)
                elif j.kind == "rows":
                    for k in range(KT):
                        mm = pe.transpose(dst[:, k * P:(k + 1) * P], h[:, k, j.arg * P:(j.arg + 1) * P], c("ident"))
                elif j.kind == "rank":
                    pe.wait_ge(group_ready.sem, group_ready.at(l, 1))
                    for i in range(TILES):
                        for i2 in range(i + 1):
                            before = c("tail", 2, P)[:, 1, :] if i2 == i else c("ones")
                            mm = pe.matmul(dst[:, i * GROUPS:(i + 1) * GROUPS], before, rt[:, 2, i2, :], start=(i2 == 0),
                                           stop=(i2 == i))
                elif j.kind == "total":
                    for i in range(TILES):
                        mm = pe.matmul(dst[:, 0:GROUPS], c("ones"), rt[:, 2, i, :], start=(i == 0), stop=(i == TILES - 1))
                elif j.kind == "place":
                    pe.wait_ge(place_ready.sem, place_ready.at(l, 1))
                    for i in range(TILES):
                        mm = pe.matmul(dst[:, i * P:(i + 1) * P], place[:, i, :].to_broadcast([P, P]), c("ident"),
                                       start=True, stop=True)
                elif j.kind == "gather":
                    if g is None:
                        pe.wait_ge(sel_ready.sem, sel_ready.at(l, 1))
                    else:
                        pe.wait_ge(sel_ready.sem, sel_ready.at(l, g + 2))
                    for k in range(KT):
                        for i in range(TILES):
                            mm = pe.matmul(dst[:, k * P:(k + 1) * P], h_rows[:, i, k * P:(k + 1) * P], sel[:, i, :],
                                           start=(i == 0), stop=(i == TILES - 1))
                elif j.kind == "weights":
                    if g is None:
                        pe.wait_ge(weight_ready.sem, weight_ready.at(l, 1))
                    for i in range(TILES):
                        mm = pe.matmul(dst[:, 0:EPG], sel[:, i, :], rt[:, 7, i, :], start=(i == 0), stop=(i == TILES - 1))
                elif j.kind in ("moe_gate", "moe_up"):
                    for ft in range(2):
                        w = unit(j.units[ft])
                        for k in range(KT):
                            mm = pe.matmul(dst[:, ft * P:(ft + 1) * P], w[:, k, :], hb[:, k, :], start=(k == 0),
                                           stop=(k == KT - 1))
                elif j.kind == "moe_down":
                    pe.wait_ge(*out_of(l, moe_at("moe_up", j.arg), g))
                    w = view(ring[:, (j.units[0] // 2) % RING, :], 0, 2, D)
                    for lo in range(0, D, 512):
                        for ft in range(2):
                            mm = pe.matmul(dst[:, lo:lo + 512], ab[:, j.arg % 2, ft, :], w[:, ft, lo:lo + 512],
                                           start=(ft == 0), stop=(ft == 1))
                elif j.kind == "back":
                    if j.arg == 0:
                        pe.wait_ge(unsort_ready.sem, unsort_ready.at(l, 1))
                        pe.wait_ge(*out_of(l, START["back"] - 1))
                    mm = product(dst, lambda k: y_blocks[:, k, j.arg * P:(j.arg + 1) * P],
                                 lambda k, a, b: unsort[:, k, a:b], NBLK)
                mm.then_inc(job_full.sem, 1)

            def run_part(l, name):
                for k, j in enumerate(PARTS[name]):
                    run_job(l, START[name] + k, j)

            def free_slots(l, n):
                pe.wait_ge(*out_of(l, n - 1))
                pe.wait_ge(*out_of(l, n - 2))

            def hgrn(l):
                def decays(u, a):
                    d, stream, i = HGRN_UNITS[u]
                    if u == 0 and a == 0:
                        pe.wait_ge(f_ready.sem, f_ready.at(l, 1))
                    if u == TILES and a == 0:
                        pe.wait_ge(f_ready.sem, f_ready.at(l, 2))
                    if u >= 1:
                        pe.wait_ge(ex_ready.sem, ex_ready.at(l, 2 * (u - 1) + a + 1))
                    for b in range(2):
                        mm = pe.matmul(ps[:, 2 * a + b, :], lf[:, i, d * BW + a * P:d * BW + (a + 1) * P],
                                       c("decay", 2, 8 * P)[:, d, b * 512:(b + 1) * 512], start=True, stop=True)
                    mm.then_inc(decay_full.sem, 1)

                def tails(u):
                    d, stream, i = HGRN_UNITS[u]
                    if u >= 1:
                        pe.wait_ge(es_ready.sem, es_ready.at(l, u))
                        pe.wait_ge(kT_ready.sem, kT_ready.at(l, u))
                    pe.matmul(ps[:, 4, 0:BW], c("tail", 2, P)[:, d, :], lf[:, i, d * BW:(d + 1) * BW], start=True,
                              stop=True)
                    for a in range(2):
                        mm = pe.transpose(ps[:, 4, BW + a * P:BW + (a + 1) * P],
                                          kk[:, i, d * BW + a * P:d * BW + (a + 1) * P], c("ident"))
                    mm.then_inc(tail_full.sem, 1)

                def scores(u, f):
                    d, stream, i = HGRN_UNITS[u]
                    v = u % 2
                    if f == 0:
                        pe.wait_ge(ke_ready.sem, ke_ready.at(l, 2 * u + 2))
                        pe.wait_ge(qe_ready.sem, qe_ready.at(l, 2 * u + 2))
                    k = FILLS * u + f
                    if k >= 1:
                        pe.wait_ge(score_out.sem, score_out.at(l, k))
                    for lev in FILL_LEVELS[f]:
                        for a in range(2):
                            for par in range(2):
                                rows = slice(HD * par, HD * (par + 1))
                                if lev == LEVELS:
                                    c0 = a * 256 + HD
                                    mm = pe.matmul(ps[:, 5 + par, c0:c0 + P], kT[v][rows, a, :],
                                                   fm[rows, HQ + a, i * P:(i + 1) * P], start=True, stop=True)
                                    continue
                                half = HD >> lev
                                q = ex[v][rows, a, lev, :].rearrange("p (n two h) -> p n two h", two=2, h=half)
                                c0 = a * 256 + (lev - FILL_LEVELS[f][0]) * HD
                                mm = pe.matmul(ps[:, 5 + par, c0:c0 + HD].rearrange("p (n h) -> p n h", h=half),
                                               ke[v][rows, a, lev, :], q[:, :, 1 - d, :], start=True, stop=True)
                    mm.then_inc(score_full.sem, 1)

                def outputs(u):
                    d, stream, i = HGRN_UNITS[u]
                    v = u % 2
                    if u >= 1:
                        pe.wait_ge(s_ready.sem, s_ready.at(l, u))
                    pe.wait_ge(kd_ready.sem, kd_ready.at(l, u + 1))
                    for e in range(HEADS):
                        a, at = e // 2, HD * (e % 2)
                        pe.matmul(ps[at:at + HD, 7, 256 + a * HD:256 + (a + 1) * HD], kd[v][:, e * HD:(e + 1) * HD],
                                  hi[:, i, e * HD:(e + 1) * HD], start=True, stop=True)
                    pe.wait_ge(score_out.sem, score_out.at(l, FILLS * (u + 1)))
                    for e in range(HEADS):
                        a, at = e // 2, HD * (e % 2)
                        pe.matmul(ps[at:at + HD, 7, a * P:(a + 1) * P], hi[:, i, e * HD:(e + 1) * HD],
                                  at_[v][:, (e % 2) * 2 + e // 2, :], start=True, stop=False)
                        mm = pe.matmul(ps[at:at + HD, 7, a * P:(a + 1) * P], st[at:at + HD, d, stream, a, :],
                                       ex[v][at:at + HD, a, 7, :], start=False, stop=True)
                    mm.then_inc(o_full.sem, 1)

                pe.wait_ge(params_loaded.sem, params_loaded.at(l, 32))
                pe.wait_ge(small_ready.sem, small_ready.at(l, 1))
                tails(0)
                decays(0, 0)
                decays(0, 1)
                for u in range(NU):
                    if u + 1 < NU:
                        tails(u + 1)
                        decays(u + 1, 0)
                    scores(u, 0)
                    if u + 1 < NU:
                        decays(u + 1, 1)
                    scores(u, 1)
                    scores(u, 2)
                    outputs(u)

            def attention(l):
                def s(u):
                    b, hd, i = ATT_UNITS[u]
                    if u >= 2:
                        pe.wait_ge(att_s_out.sem, att_s_out.at(l, u - 1))
                    dst = banks(2 * (u % 2), 2)
                    if b == "na":
                        at, q, k, ck = HD * (hd % 2), NAQ + hd // 2, NAK + hd // 2, pa("nk", 2, P)[:, hd // 2, :]
                    else:
                        at, q, k, ck = HD * (hd // 2), SQ + hd % 2, SK, pa("sk")
                    lo, hi_ = key_range(b, i)
                    qs = fm[at:at + HD, q, i * P:(i + 1) * P]
                    mm = pe.matmul(dst[:, 0:hi_ - lo], qs, fm[at:at + HD, k, lo:hi_], start=True, stop=True)
                    if i < LT:
                        mm = pe.matmul(dst[:, hi_ - lo:hi_ - lo + P], qs, ck[at:at + HD, :], start=True, stop=True)
                    mm.then_inc(att_s_full.sem, 1)

                def t(u):
                    b, hd, i = ATT_UNITS[u]
                    pe.wait_ge(att_p.sem, att_p.at(l, u + 1))
                    if u >= 1:
                        pe.wait_ge(att_t_out.sem, att_t_out.at(l, u))
                    for k in range(n_keys(b, i) // P):
                        mm = pe.transpose(banks(4, 2)[:, k * P:(k + 1) * P], sbs[:, u % 3, k * P:(k + 1) * P], c("ident"))
                    mm.then_inc(att_t_full.sem, 1)

                def pv(u):
                    b, hd, i = ATT_UNITS[u]
                    pe.wait_ge(att_t_out.sem, att_t_out.at(l, u + 1))
                    if u >= 2:
                        pe.wait_ge(att_o_out.sem, att_o_out.at(l, u - 1))
                    lo, hi_ = key_range(b, i)
                    if b == "na":
                        at, v, cv, cols = HD * (hd % 2), nav, pa("nv"), slice(hd * HD, (hd + 1) * HD)
                    else:
                        at, v, cv, cols = HD * (hd // 2), sv, pa("sv"), slice((hd // 2) * HD, (hd // 2 + 1) * HD)
                    n = n_keys(b, i) // P
                    for k in range(n):
                        w = cv[:, cols] if lo + k * P >= hi_ else v[:, lo // P + k, cols]
                        mm = pe.matmul(ps[at:at + HD, 6 + u % 2, 0:P], w, pts[:, u % 2, k * P:(k + 1) * P],
                                       start=(k == 0), stop=(k == n - 1))
                    mm.then_inc(att_o_full.sem, 1)

                for step in range(-2, NAT + 1):
                    if step + 2 < NAT:
                        s(step + 2)
                    if 0 <= step - 1:
                        pv(step - 1)
                    if 0 <= step < NAT:
                        t(step)

            def router(l):
                for i in range(TILES):
                    for k in range(KT):
                        if i == 0:
                            pe.wait_ge(h_ready.sem, h_ready.at(l, KT + k + 1))
                        mm = pe.matmul(ps[:, 6, i * 20:(i + 1) * 20], h[:, k, i * P:(i + 1) * P],
                                       pb("wr", KT, 20)[:, k, :], start=(k == 0), stop=(k == KT - 1))
                mm.then_inc(router_full.sem, 1)

            pe.wait_ge(cond_ready, 1)
            with pe.Fori(0, DEPTH) as l:
                arrived_pairs.clear()
                for k, j in enumerate(PARTS["ada"]):
                    if k == ADA_BEFORE_STATS:
                        pe.wait_ge(loaded, 16 * n_loads)
                        stats(l, 0)
                    run_job(l, START["ada"] + k, j)
                pe.wait_ge(h_ready.sem, h_ready.at(l, KT))
                run_part(l, "hgrn_in")
                free_slots(l, START["hgrn_out"])
                hgrn(l)
                run_part(l, "hgrn_out")
                run_part(l, "mix_in")
                free_slots(l, START["merge"])
                attention(l)
                run_part(l, "merge")
                run_part(l, "out")
                stats(l, 1)
                router(l)
                run_part(l, "sort")
                seen = set(arrived_pairs)
                with pe.Fori(0, NBLK - 1) as g:
                    arrived_pairs.clear()
                    for k, j in enumerate(PARTS["moe"]):
                        run_job(l, START["moe"] + k, j, g)
                arrived_pairs.clear()
                for k, j in enumerate(PARTS["moe_last"]):
                    run_job(l, START["moe"] + k, j, NBLK - 1)
                arrived_pairs |= seen
                run_part(l, "back")
            stats(DEPTH, 0)

        @block.scalar
        def _(act):
            own = Own(act, own_sem["act"], *OWN_STEPS["act"])
            act.dma_start(cond[:, :, :], A["cT"]).then_inc(c_loaded, 16)
            act.dma_start(lbraw, A["lbr"]).then_inc(lb_diff, 16)
            act.dma_start(lpb[:, :, :], A["lpb"]).then_inc(loaded, 16)
            act.dma_start(x[:, :, :], A["xT"]).then_inc(x_loaded, 16)
            for dst, src in ((cst[:, :], A["cst"]), (mraw, A["msk"]), (fg[:, :], A["fg"])):
                act.dma_start(dst, src).then_inc(loaded, 16)
            act.wait_ge(c_loaded, 16)
            act.activation(cneg[:, :, :], cond[:, :, :], ACT.Exp, scale=-1.0).then_inc(start_exp, 1)
            act.wait_ge(lb_diff, 17)
            act.activation(lbs[:, 1, :], lbs[:, 1, :], ACT.Exp).then_inc(start_exp, 1)
            act.wait_ge(cond_ready, 1)
            act.wait_ge(x_loaded, 16)

            def norm(l, k):
                for kt in range(KT):
                    if k == 1:
                        act.wait_ge(*out_of(l, job_at("out", "out", kt)))
                    elif kt == 0:
                        for s in range(2):
                            act.wait_ge(job_out[s].sem, job_out[s].at(l, 0))
                    if kt >= 2:
                        act.wait_ge(sq_used.sem, sq_used.at(l, k * KT + kt - 1))
                    act.activation(nsq[:, kt % 2, :], x[:, kt, :], ACT.Square).then_inc(sq_ready.sem, 1)
                act.wait_ge(sq_used.sem, sq_used.at(l, (k + 1) * KT))
                act.activation(rs, banks(4, 2)[:, 0:T], ACT.Ln, bias=eps[:, 0:1], scale=1.0 / D).then_inc(*own.step())
                act.wait_ge(*own.last)
                act.activation(rs, rs, ACT.Exp, scale=-0.5).then_inc(*own.tell(rs_ready, rs_ready.at(l, k + 1)))

            def modulate(l, k):
                act.wait_ge(mod_full.sem, mod_full.at(l, k + 1))
                for kt in range(KT):
                    act.wait_ge(xn_ready.sem, xn_ready.at(l, k * KT + kt + 1))
                    for w, lo, hi_ in ((0, 0, LAT), (1, LAT, T)):
                        ins = act.activation(h[:, kt, lo:hi_], xn[:, kt % 2, lo:hi_], ACT.Identity,
                                             bias=mod[:, 24 * k + kt, w:w + 1], scale=amul[:, k, kt, w:w + 1])
                    ins.then_inc(h_ready.sem, 1)

            def run_job(l, n, j, g=None):
                src = slot(n)[:, 0:T]
                if j.kind == "fm":
                    name, dst, _ = j.arg
                    act.wait_ge(*full(l, n))
                    if name in ("hq", "hog"):
                        act.activation(fm[:, dst, :], src, ACT.Exp, scale=-1.0).then_inc(neg_exp.sem, 1)
                        return
                    scale = HD ** -0.5 if name in ("naq", "sq") else 1.0
                    act.activation(fm[:, dst, :], src, ACT.Copy, scale=scale).then_inc(job_out[n % 2].sem, 1)
                elif j.kind == "tm":
                    name, i0, i1, wide = j.arg
                    act.wait_ge(*full(l, n))
                    if name == "nav" and i0 == 0:
                        act.wait_ge(o_full.sem, o_full.at(l, NU))
                    src = slot(n)[:, 0:(i1 - i0) * wide].rearrange("p (i w) -> p i w", w=wide)
                    fn, scale = (ACT.Exp, -1.0) if name in ("hff", "hfb") else (ACT.Copy, 1.0)
                    act.activation(TM_DST[name][:, i0:i1, :], src, fn, scale=scale).then_inc(job_out[n % 2].sem, 1)
                elif j.kind == "gate":
                    d, nb_ = j.arg
                    act.wait_ge(*full(l, n))
                    k = 4 * d + nb_
                    if k >= 2:
                        act.wait_ge(*out_of(l, job_at("merge", "proj", ((k - 2) // 4, (k - 2) % 4))))
                    act.activation(sg[:, nb_ % 2, :], src, ACT.Sigmoid).then_inc(job_out[n % 2].sem, 1)
                elif j.kind == "rows":
                    act.wait_ge(*full(l, n))
                    act.activation(h_rows[:, j.arg, :], slot(n), ACT.Copy).then_inc(job_out[n % 2].sem, 1)
                elif j.kind == "place":
                    act.wait_ge(*full(l, n))
                    act.activation(place_row, src, ACT.Copy).then_inc(job_out[n % 2].sem, 1)
                elif j.kind == "gather":
                    act.wait_ge(*full(l, n, g))
                    act.activation(hb[:, :, :].rearrange("p k t -> p (k t)"), slot(n), ACT.Copy).then_inc(job_out[n % 2].sem, 1)
                elif j.kind == "moe_gate":
                    act.wait_ge(*full(l, n, g))
                    act.activation(sgb[:, j.arg % 2, :], slot(n)[:, 0:2 * P], ACT.Silu).then_inc(job_out[n % 2].sem, 1)

            def logs(l, d):
                act.wait_ge(ln_in.sem, ln_in.at(l, d + 1))
                act.activation(lnb[:, d, :, :], lnb[:, d, :, :], ACT.Ln).then_inc(*own.step())
                v = lf[:, :, d * BW:(d + 1) * BW]
                act.activation(v, v, ACT.Ln).then_inc(ln_out.sem, 1)

            def hgrn(l):
                for u in range(NU):
                    v = u % 2
                    if u >= 2:
                        act.wait_ge(o_full.sem, o_full.at(l, u - 1))
                    for a in range(2):
                        act.wait_ge(decay_full.sem, decay_full.at(l, 2 * u + a + 1))
                        act.activation(ex[v][:, a, :, :], banks(2 * a, 2).rearrange("p (k t) -> p k t", k=8),
                                       ACT.Exp).then_inc(ex_ready.sem, 1)
                        if a == 0:
                            act.wait_ge(kT_ready.sem, kT_ready.at(l, u + 1))
                            act.activation(es[v], ps[:, 4, 0:BW], ACT.Exp).then_inc(es_ready.sem, 1)
                act.wait_ge(s_ready.sem, s_ready.at(l, NU))
                act.dma_start(A["st_out"][l], st[:, :, 0, :, :]).then_inc(kv_out.sem, 16)

            def hgrn_norm(l):
                act.wait_ge(o_full.sem, o_full.at(l, NU))
                for a in range(2):
                    act.activation(osq[:, a, :], o[:, a, :], ACT.Square).then_inc(osq_ready.sem, 1)
                for a in range(2):
                    n = START["hgrn_out"] + a
                    act.wait_ge(*full(l, n))
                    act.activation(ors[:, a, :], slot(n)[:, 0:T], ACT.Ln, bias=eps[:, 0:1], scale=1.0 / HD).then_inc(*own.step())
                    act.wait_ge(*own.last)
                    act.activation(ors[:, a, :], ors[:, a, :], ACT.Exp, scale=-0.5).then_inc(job_out[n % 2].sem, 1)

            def attention(l):
                for step in range(-2, NAT + 1):
                    u = step + 1
                    if 0 <= u < NAT:
                        b, hd, i = ATT_UNITS[u]
                        n = n_keys(b, i) + (b == "swa")
                        act.wait_ge(att_s_out.sem, att_s_out.at(l, u + 1))
                        if u >= 3:
                            act.wait_ge(att_rinv.sem, att_rinv.at(l, u - 2))
                        act.activation(sbs[:, u % 3, 0:n], sbs[:, u % 3, 0:n], ACT.Exp, bias=nmx[:, u % 3:u % 3 + 1],
                                       accum_out=sums[:, u % 3:u % 3 + 1]).then_inc(att_exp.sem, 1)
                    u = step
                    if 0 <= u < NAT:
                        b, hd, i = ATT_UNITS[u]
                        act.wait_ge(att_t_full.sem, att_t_full.at(l, u + 1))
                        if u >= 2:
                            act.wait_ge(att_o_full.sem, att_o_full.at(l, u - 1))
                        n = n_keys(b, i)
                        act.activation(pts[:, u % 2, 0:n], banks(4, 2)[:, 0:n], ACT.Copy).then_inc(att_t_out.sem, 1)

            with act.Fori(0, DEPTH) as l:
                own.layer(l)
                norm(l, 0)
                act.dma_start(lpa[:, :], A["lpa"][l]).then_inc(params_loaded.sem, 16)
                act.dma_start(st[:, :, 1, :, :], A["st_in"][l]).then_inc(params_loaded.sem, 16)
                modulate(l, 0)
                for k, j in enumerate(PARTS["hgrn_in"]):
                    run_job(l, START["hgrn_in"] + k, j)
                    if j.kind == "tm" and j.arg[0:2] == ("hi", LT):
                        logs(l, 0)
                        logs(l, 1)
                act.wait_ge(f_ready.sem, f_ready.at(l, 2))
                hgrn(l)
                hgrn_norm(l)
                for k, j in enumerate(PARTS["mix_in"]):
                    run_job(l, START["mix_in"] + k, j)
                    if j.kind == "tm" and j.arg[0:2] == ("mv", LT):
                        act.wait_ge(v_stat.sem, v_stat.at(l, 1))
                        act.activation(vstat[:, :], vstat[:, :], ACT.Ln, bias=eps[:, 0:1], scale=1.0 / HD).then_inc(*own.step())
                        act.wait_ge(*own.last)
                        act.activation(vstat[:, :], vstat[:, :], ACT.Exp, scale=-0.5).then_inc(v_rs.sem, 1)
                kv_jobs = [job_at("mix_in", "fm", t) for t in (("sk", SK), ("nak", NAK), ("nak", NAK + 1))]
                kv_jobs += [job_at("mix_in", "tm", (t, LT)) for t in ("nav", "sv")]
                act.wait_ge(*out_of(l, max(n for n in kv_jobs if n % 2 == 0)))
                act.wait_ge(*out_of(l, max(n for n in kv_jobs if n % 2 == 1)))
                act.dma_start(A["nk_out"][l], fm[:, NAK:NAK + 2, LAT:T]).then_inc(kv_out.sem, 16)
                act.dma_start(A["nv_out"][l], nav[:, CT, :]).then_inc(kv_out.sem, 16)
                act.dma_start(A["sk_out"][l], fm[:, SK, LAT:T]).then_inc(kv_out.sem, 16)
                act.dma_start(A["sv_out"][l], sv[:, CT, :]).then_inc(kv_out.sem, 16)
                attention(l)
                for k, j in enumerate(PARTS["merge"]):
                    run_job(l, START["merge"] + k, j)
                norm(l, 1)
                modulate(l, 1)
                for k, j in enumerate(PARTS["sort"]):
                    if j.kind in ("place", "gather"):
                        r = int(j.kind == "gather")
                        act.wait_ge(r_in.sem, r_in.at(l, r + 1))
                        v = rt[:, 12 + r, :, 0:1 if r else 4]
                        act.activation(v, v, ACT.Exp).then_inc(r_exp.sem, 1)
                    run_job(l, START["sort"] + k, j)
                with act.Fori(0, NBLK - 1) as g:
                    for k, j in enumerate(PARTS["moe"]):
                        run_job(l, START["moe"] + k, j, g)
                for k, j in enumerate(PARTS["moe_last"]):
                    run_job(l, START["moe"] + k, j, NBLK - 1)
                own.end_layer()
            own.layer(DEPTH)
            norm(DEPTH, 0)
            for kt in range(KT):
                act.wait_ge(xn_ready.sem, xn_ready.at(DEPTH, kt + 1))
                act.activation(h[:, kt, :], xn[:, kt % 2, :], ACT.Copy, scale=fg[:, kt:kt + 1])\
                   .then_inc(h_ready.sem, 1)
            act.wait_ge(kv_out.sem, kv_out.at(DEPTH, 0))

        @block.vector
        def _(dve):
            own = Own(dve, own_sem["dve"], *OWN_STEPS["dve"])
            own.layer(0)
            head = start_steps
            n_head = [0]

            def first(ins):
                n_head[0] += 1
                ins.then_inc(head, 1)
                dve.wait_ge(head, n_head[0])

            for s in range(2):
                dve.sem_inc(job_out[s].sem)
            dve.memset(eps[:, :], EPS).then_inc(head, 1)
            n_head[0] += 1
            dve.wait_ge(lb_diff, 16)
            dve.tensor_tensor(lbs[:, 1, :], lbraw[:, 0, :], lbraw[:, 1, :], ALU.subtract).then_inc(lb_diff, 1)
            dve.memset(lbs[:, 0, :], 0.0).then_inc(head, 1)
            n_head[0] += 1
            dve.wait_ge(start_exp, 2)
            first(dve.tensor_scalar(lbs[:, 1, :], lbs[:, 1, :], 1.0, None, ALU.add))
            first(dve.reciprocal(lbs[:, 1, :], lbs[:, 1, :]))
            first(dve.tensor_scalar(cneg[:, :, :], cneg[:, :, :], 1.0, None, ALU.add))
            first(dve.reciprocal(cneg[:, :, :], cneg[:, :, :]))
            dve.tensor_tensor(cond[:, :, :], cond[:, :, :], cneg[:, :, :], ALU.mult).then_inc(cond_ready, 1)


            def norm_x(l, k):
                dve.wait_ge(rs_ready.sem, rs_ready.at(l, k + 1))
                for kt in range(KT):
                    if kt >= 2:
                        dve.wait_ge(h_ready.sem, h_ready.at(l, k * KT + kt - 1))
                    dve.tensor_tensor(xn[:, kt % 2, :], x[:, kt, :], rs, ALU.mult).then_inc(*own.tell(xn_ready, xn_ready.at(l, k * KT + kt + 1)))

            def gain(l, k):
                name = ("n1", "n2")[k]
                dve.wait_ge(*own.last)
                g = pb(name).unsqueeze(2).to_broadcast([P, KT, 2])
                dve.scalar_tensor_tensor(out=amul[:, k, :, :], in0=mod[:, 24 * k + 8:24 * k + 16, :],
                                                  scalar=1.0, in1=g, op0=ALU.add, op1=ALU.mult).then_inc(*own.tell(mod_full, mod_full.at(l, k + 1)))

            def residual(l, n, g, d, first_unit):
                for w, lo, hi_ in ((0, 0, LAT), (1, LAT, T)):
                    ins = dve.scalar_tensor_tensor(
                        out=x[:, d, lo:hi_], in0=slot(n)[:, lo:hi_], scalar=mod[:, first_unit + d, w:w + 1],
                        in1=x[:, d, lo:hi_], op0=ALU.mult, op1=ALU.add)
                    if w == 0:
                        ins.then_inc(*own.step())
                ins.then_inc(*own.tell(*out_at(l, n, g)))

            def run_job(l, n, j, g=None):
                src = slot(n)[:, 0:T]
                if j.kind == "ada":
                    i = j.arg
                    dve.wait_ge(*full(l, n))
                    b = pb("b_ada")[:, 2 * i:2 * i + 2].unsqueeze(2).to_broadcast([P, 2, 2])
                    dve.tensor_tensor(mod[:, 2 * i:2 * i + 2, :], slot(n)[:, 0:4].rearrange("p (u w) -> p u w", w=2), b, ALU.add).then_inc(*own.tell(*out_at(l, n)))
                    if i == 7:
                        gain(l, 0)
                    if i == 19:
                        gain(l, 1)
                elif j.kind == "fm" and j.arg[0] in ("hq", "hog"):
                    name, dst, _ = j.arg
                    k = (dst - HQ if name == "hq" else 2 + dst - HOG)
                    dve.wait_ge(neg_exp.sem, neg_exp.at(l, k + 1))
                    v = fm[:, dst, :]
                    dve.tensor_scalar(v, v, 1.0, None, ALU.add).then_inc(*own.step())
                    dve.wait_ge(*own.last)
                    dve.reciprocal(v, v).then_inc(*own.step())
                    dve.wait_ge(*own.last)
                    dve.tensor_tensor(v, v, src, ALU.mult).then_inc(*own.tell(*out_at(l, n)))
                elif j.kind == "rope":
                    a = j.arg
                    v = fm[:, a, 0:LAT]
                    dve.wait_ge(*full(l, n))
                    dve.tensor_tensor(v, v, c("cos"), ALU.mult).then_inc(*own.step())
                    dve.tensor_tensor(slot(n)[:, 0:LAT], slot(n)[:, 0:LAT], c("sin"), ALU.mult).then_inc(*own.step())
                    dve.wait_ge(*own.last)
                    dve.tensor_tensor(v, v, slot(n)[:, 0:LAT], ALU.add).then_inc(*own.tell(*out_at(l, n)))
                elif j.kind == "mlp":
                    a = j.arg
                    dve.wait_ge(*full(l, n))
                    dve.wait_ge(*out_of(l, job_at("mix_in", "fm", ("mu", MU + a))))
                    b = pa("smb", 2, P)[:, a, :].unsqueeze(1).to_broadcast([P, TILES, P])
                    s3 = src.rearrange("p (i t) -> p i t", t=P)
                    dve.tensor_tensor(s3, s3, b, ALU.add).then_inc(*own.step())
                    dve.wait_ge(*own.last)
                    dve.tensor_tensor(fm[:, MU + a, :], fm[:, MU + a, :], src, ALU.mult).then_inc(*own.tell(*out_at(l, n)))
                elif j.kind == "proj":
                    d, nb_ = j.arg
                    dve.wait_ge(*full(l, n))
                    dve.wait_ge(*out_of(l, n - 1))
                    if nb_ == 0:
                        dve.tensor_tensor(merged[:, d, :], src, sg[:, 0, :], ALU.mult).then_inc(*own.tell(*out_at(l, n)))
                        return
                    dve.tensor_tensor(mt[:, nb_ % 2, :], src, sg[:, nb_ % 2, :], ALU.mult).then_inc(*own.tell(*out_at(l, n)))
                    dve.wait_ge(*own.last)
                    dve.tensor_tensor(merged[:, d, :], merged[:, d, :], mt[:, nb_ % 2, :], ALU.add)\
                       .then_inc(*(own.tell(m_ready, m_ready.at(l, d + 1)) if nb_ == NB - 1 else own.step()))
                elif j.kind == "out":
                    dve.wait_ge(*full(l, n))
                    residual(l, n, None, j.arg, 16)
                elif j.kind == "weights":
                    dve.wait_ge(*full(l, n, g))
                    dve.wait_ge(*own.last)
                    dve.tensor_copy(cs[:, :], slot(n)[:, 0:EPG]).then_inc(*own.tell(*out_at(l, n, g)))
                elif j.kind == "moe_up":
                    e = j.arg
                    dve.wait_ge(*full(l, n, g))
                    dve.wait_ge(*out_of(l, moe_at("moe_gate", e), g))
                    dve.tensor_tensor(ab[:, e % 2, :, :], slot(n)[:, 0:2 * P].rearrange("p (f t) -> p f t", f=2),
                                      sgb[:, e % 2, :].rearrange("p (f t) -> p f t", f=2), ALU.mult)\
                       .then_inc(*own.tell(*out_at(l, n, g)))
                elif j.kind == "moe_down":
                    e = j.arg
                    y = y_blocks[:, g, :]
                    dve.wait_ge(*full(l, n, g))
                    dve.wait_ge(*own.last)
                    if e == 0:
                        dve.tensor_scalar(y, slot(n), cs[:, 0:1], None, ALU.mult).then_inc(*own.tell(*out_at(l, n, g)))
                    else:
                        dve.scalar_tensor_tensor(out=y, in0=slot(n), scalar=cs[:, e:e + 1], in1=y, op0=ALU.mult,
                                                 op1=ALU.add).then_inc(*own.tell(*out_at(l, n, g)))
                elif j.kind == "back":
                    dve.wait_ge(*full(l, n))
                    residual(l, n, None, j.arg, 40)

            def select(l, b):
                wide = [P, TILES, P]
                dve.tensor_tensor(sel, ahead[:, :, :].to_broadcast(wide), c("iota").unsqueeze(1).to_broadcast(wide),
                                  ALU.is_equal).then_inc(*own.tell(sel_ready, sel_ready.at(l, b + 1)))

            def block(l, g, jobs):
                if jobs is PARTS["moe"]:
                    dve.tensor_scalar(ahead[:, :, :], ahead[:, :, :], -float(P), None, ALU.add).then_inc(*own.step())
                    dve.wait_ge(*own.last)
                    select(l, g + 1)
                for k, j in enumerate(jobs):
                    run_job(l, START["moe"] + k, j, g)

            def sort(l):
                og = rt[:, 2, :, :]
                four = [P, TILES, 4]
                dve.wait_ge(*full(l, START["sort"] + TILES))
                dve.tensor_copy(rank[:, :, :], slot(START["sort"] + TILES)[:, 0:TILES * GROUPS].rearrange(
                    "p (i g) -> p i g", g=GROUPS)).then_inc(*own.tell(*out_at(l, START["sort"] + TILES)))
                n = START["sort"] + TILES + 1
                total = slot(n)[:, 0:GROUPS]
                dve.wait_ge(*full(l, n))
                dve.tensor_scalar(n_blocks[:, :], total, float(P), 1.0, ALU.is_gt, ALU.add).then_inc(*own.step())
                for k in range(2, TILES):
                    dve.wait_ge(*own.last)
                    dve.scalar_tensor_tensor(out=n_blocks[:, :], in0=total, scalar=float(k * P), in1=n_blocks[:, :],
                                             op0=ALU.is_gt, op1=ALU.add)\
                       .then_inc(*(own.tell(*out_at(l, n)) if k == TILES - 1 else own.step()))
                dve.wait_ge(*own.last)
                dve.tensor_copy(end_block[:, 0:1], n_blocks[:, 0:1]).then_inc(*own.step())
                for k in range(1, GROUPS):
                    dve.wait_ge(*own.last)
                    dve.tensor_tensor(end_block[:, k:k + 1], end_block[:, k - 1:k], n_blocks[:, k:k + 1], ALU.add).then_inc(*own.step())
                dve.wait_ge(*own.last)
                dve.tensor_tensor(first_slot[:, :], end_block[:, :], n_blocks[:, :], ALU.subtract).then_inc(*own.step())
                of, is_after = group_of[:, 0, :], group_of[:, 1, :]
                ids = c("blockid")
                dve.tensor_tensor(of, ids, end_block[:, 0:1].to_broadcast([P, NBLK]), ALU.is_ge).then_inc(*own.step())
                for k in range(1, GROUPS - 1):
                    dve.tensor_tensor(is_after, ids, end_block[:, k:k + 1].to_broadcast([P, NBLK]), ALU.is_ge).then_inc(*own.step())
                    dve.wait_ge(*own.last)
                    dve.tensor_tensor(of, of, is_after, ALU.add).then_inc(*own.step())
                    dve.wait_ge(*own.last)
                dve.tensor_copy(table[:, :], of).then_inc(*own.tell(table_ready, table_ready.at(l, 1)))
                dve.tensor_scalar(first_slot[:, :], first_slot[:, :], float(P), None, ALU.mult).then_inc(*own.step())
                dve.wait_ge(*own.last)
                dve.tensor_tensor(rank[:, :, :], rank[:, :, :], first_slot[:, :].unsqueeze(1).to_broadcast(four), ALU.add).then_inc(*own.step())
                dve.wait_ge(*own.last)
                dve.tensor_tensor(rank[:, :, :], rank[:, :, :], og, ALU.mult).then_inc(*own.step())
                dve.wait_ge(*own.last)
                dve.tensor_reduce(place[:, :, :], rank[:, :, :], AX.X, ALU.add).then_inc(*own.tell(place_ready, place_ready.at(l, 1)))
                dve.wait_ge(*own.last)
                dve.tensor_copy(ahead[:, :, :], place[:, :, :]).then_inc(*own.step())
                dve.wait_ge(*own.last)
                select(l, 0)

            def unsorting(l):
                dve.wait_ge(*out_of(l, START["sort"] + TILES + 2))
                dve.wait_ge(*out_of(l, START["sort"] + TILES - 1))
                for b in range(NBLK):
                    ins = dve.tensor_tensor(unsort[:, b, :], place_row, c("slotid")[:, b:b + 1].to_broadcast([P, T]),
                                            ALU.is_equal)
                    if b < NBLK - 1:
                        ins.then_inc(*own.step())
                ins.then_inc(*own.tell(unsort_ready, unsort_ready.at(l, 1)))

            def sum_ada(l, j):
                pair = j.units[0] // 2
                w = view(ring[:, pair % RING, :], 0, 2, KT, P)
                dve.wait_ge(arrived[pair % RING].sem, arrived[pair % RING].at(l, 16 * (pair // RING + 1)))
                alone(dve)
                for k in range(KT):
                    dve.wait_ge(*own.last)
                    for s_ in range(2):
                        acc = ada_sums[:, s_, :].rearrange("p (u m) -> p u m", u=2)
                        if k == 0:
                            ins = dve.tensor_scalar(acc, w[:, :, k, :], cond[:, k, s_:s_ + 1], None, ALU.mult)
                        else:
                            ins = dve.scalar_tensor_tensor(out=acc, in0=w[:, :, k, :], scalar=cond[:, k, s_:s_ + 1],
                                                           in1=acc, op0=ALU.mult, op1=ALU.add)
                        if k < KT - 1 or s_ == 0:
                            ins.then_inc(*own.step())
                ins.then_inc(*own.tell(sums_ready, sums_ready.at(l, j.arg - FIRST_DVE_ADA + 1)))

            def forget(l, d):
                n = job_at("hgrn_in", "tm", (("hff", "hfb")[d], LT))
                dve.wait_ge(*out_of(l, n))
                dve.wait_ge(*out_of(l, n - 1))
                cols = slice(d * BW, (d + 1) * BW)
                k, f, b = kk[:, :, cols], lf[:, :, cols], lnb[:, d, :, :]
                wide = [P, TILES, BW]
                dve.tensor_scalar(k, k, 1.0, None, ALU.add).then_inc(*own.step())
                dve.wait_ge(*own.last)
                dve.reciprocal(k, k).then_inc(*own.step())
                dve.wait_ge(*own.last)
                dve.tensor_tensor(f, k, omlb[:, cols].unsqueeze(1).to_broadcast(wide), ALU.mult).then_inc(*own.step())
                dve.wait_ge(*own.last)
                dve.tensor_tensor(f, f, lbs[:, l, cols].unsqueeze(1).to_broadcast(wide), ALU.add).then_inc(*own.step())
                dve.wait_ge(*own.last)
                dve.tensor_scalar(k, f, -1.0, 1.0, ALU.mult, ALU.add).then_inc(*own.step())
                dve.tensor_scalar(b, f, LN_SPLIT, 1.0, ALU.mult, ALU.min).then_inc(*own.step())
                dve.wait_ge(*own.last)
                dve.tensor_scalar(b, b, TINY * LN_SPLIT, None, ALU.max).then_inc(*own.step())
                dve.tensor_scalar(f, f, 1.0 / LN_SPLIT, None, ALU.max).then_inc(*own.tell(ln_in, ln_in.at(l, d + 1)))

            def hgrn(l):
                def keys(u):
                    dve.wait_ge(tail_full.sem, tail_full.at(l, u + 1))
                    if u >= 2:
                        dve.wait_ge(o_full.sem, o_full.at(l, u - 1))
                    dve.tensor_copy(kT[u % 2], ps[:, 4, BW:2 * BW].rearrange("p (a s) -> p a s", a=2)).then_inc(*own.tell(kT_ready, kT_ready.at(l, u + 1)))
                    if u % TILES < 2:
                        dve.memset(at_[u % 2], 0.0).then_inc(*own.step())

                def queries(u, a):
                    d, stream, i = HGRN_UNITS[u]
                    v = u % 2
                    dve.wait_ge(ke_ready.sem, ke_ready.at(l, 2 * u + a + 1))
                    last = 127 if d == 0 else 0
                    dve.tensor_copy(tot[:, v, a:a + 1], ex[v][:, a, 7, last:last + 1]).then_inc(*own.step())
                    dve.wait_ge(*own.last)
                    q = fm[:, HQ + a, i * P:(i + 1) * P].unsqueeze(1).to_broadcast([P, 8, P])
                    dve.tensor_tensor(ex[v][:, a, :, :], ex[v][:, a, :, :], q, ALU.mult).then_inc(*own.tell(qe_ready, qe_ready.at(l, 2 * u + a + 1)))

                def take_scores(u, f):
                    d, stream, i = HGRN_UNITS[u]
                    v = u % 2
                    k = FILLS * u + f
                    dve.wait_ge(*own.last)
                    dve.wait_ge(score_full.sem, score_full.at(l, k + 1))
                    alone(dve)
                    both = banks(5, 2).rearrange("p (e c) -> p e c", e=HEADS)
                    for lev in FILL_LEVELS[f]:
                        if lev != FILL_LEVELS[f][0]:
                            dve.wait_ge(*own.last)
                            alone(dve)
                        if lev == LEVELS:
                            m = c("ident").bitcast(mybir.dt.int32).unsqueeze(1).to_broadcast([P, HEADS, P])
                            ins = dve.copy_predicated(at_[v], m, both[:, :, HD:HD + P])
                        else:
                            half = HD >> lev
                            dst = at_[v].rearrange("p e (n two h) -> p e n two h", two=2, h=half)[:, :, :, 1 - d, :]
                            m = msk[:, d, lev, :].rearrange("p (n h) -> p n h", h=half).unsqueeze(1)\
                                .to_broadcast([P, HEADS, HD // half, half])
                            c0 = (lev - FILL_LEVELS[f][0]) * HD
                            ins = dve.copy_predicated(dst, m, both[:, :, c0:c0 + HD].rearrange(
                                "p e (n h) -> p e n h", h=half))
                        if lev == FILL_LEVELS[f][-1]:
                            ins.then_inc(*own.tell(score_out, score_out.at(l, k + 1)))
                        else:
                            ins.then_inc(*own.step())

                def results(u):
                    d, stream, i = HGRN_UNITS[u]
                    dve.wait_ge(o_full.sem, o_full.at(l, u + 1))
                    src = ps[:, 7, 0:BW].rearrange("p (a t) -> p a t", a=2)
                    dst = o[:, :, i * P:(i + 1) * P]
                    if d == 0:
                        dve.tensor_copy(dst, src).then_inc(*own.step())
                    else:
                        dve.tensor_tensor(dst, dst, src, ALU.add).then_inc(*own.step())
                    for a in range(2):
                        ins = dve.scalar_tensor_tensor(
                            out=st[:, d, stream, a, :], in0=st[:, d, stream, a, :], scalar=tot[:, u % 2, a:a + 1],
                            in1=ps[:, 7, 256 + a * HD:256 + (a + 1) * HD], op0=ALU.mult, op1=ALU.add)
                        if a == 0:
                            ins.then_inc(*own.step())
                    ins.then_inc(*own.tell(s_ready, s_ready.at(l, u + 1)))

                keys(0)
                queries(0, 0)
                queries(0, 1)
                for u in range(NU):
                    if u + 1 < NU:
                        keys(u + 1)
                    take_scores(u, 0)
                    take_scores(u, 1)
                    take_scores(u, 2)
                    if u + 1 < NU:
                        queries(u + 1, 0)
                        queries(u + 1, 1)
                    results(u)

            def hgrn_norm(l):
                for a in range(2):
                    dve.wait_ge(*out_of(l, START["hgrn_out"] + a))
                    v = o[:, a, :]
                    dve.tensor_tensor(v, v, ors[:, a, :], ALU.mult).then_inc(*own.step())
                    dve.wait_ge(*own.last)
                    dve.scalar_tensor_tensor(out=fm[:, HQ + a, :], in0=v, scalar=pb("on")[:, a:a + 1],
                                                      in1=fm[:, HOG + a, :], op0=ALU.mult, op1=ALU.mult).then_inc(*own.tell(a_done, a_done.at(l, a + 1)))

            def mlp_norm(l):
                dve.wait_ge(*out_of(l, job_at("mix_in", "tm", ("mv", 0))))
                dve.wait_ge(*out_of(l, job_at("mix_in", "tm", ("mv", LT))))
                dve.tensor_tensor(mvsq, mv, mv, ALU.mult).then_inc(*own.step())
                dve.wait_ge(*own.last)
                dve.tensor_reduce(vstat[:, :], mvsq.rearrange("p i (g c) -> p (i g) c", c=HD), AX.X, ALU.add).then_inc(*own.tell(v_stat, v_stat.at(l, 1)))
                dve.wait_ge(v_rs.sem, v_rs.at(l, 1))
                v = mv.rearrange("p i (g c) -> p (i g) c", c=HD)
                dve.tensor_tensor(v, v, vstat[:, :].unsqueeze(2).to_broadcast([P, 20, HD]), ALU.mult).then_inc(*own.tell(v_ready, v_ready.at(l, 1)))

            def attention(l):
                for step in range(-2, NAT + 1):
                    u = step + 2
                    if u < NAT:
                        b, hd, i = ATT_UNITS[u]
                        lo, hi_ = key_range(b, i)
                        n = hi_ - lo
                        dve.wait_ge(att_s_full.sem, att_s_full.at(l, u + 1))
                        if u >= 3:
                            dve.wait_ge(att_t_full.sem, att_t_full.at(l, u - 2))
                        src, dst = banks(2 * (u % 2), 2), sbs[:, u % 3, :]
                        if i == CT:
                            dve.tensor_copy(dst[:, 0:n], src[:, 0:n]).then_inc(*own.step())
                        else:
                            if b == "na":
                                e0 = (6 - 2 * i) * HD
                                bias = nab[:, hd, e0:e0 + LAT]
                            else:
                                m0 = P if i == 0 else 0
                                bias = c("swm")[:, m0:m0 + n]
                            dve.tensor_tensor(dst[:, 0:n], src[:, 0:n], bias, ALU.add).then_inc(*own.step())
                            dve.tensor_copy(dst[:, n:n + P], src[:, n:n + P]).then_inc(*own.step())
                            n += P
                        if b == "swa":
                            dve.tensor_copy(dst[:, n:n + 1], pa("sink")[:, hd:hd + 1]).then_inc(*own.step())
                            n += 1
                        dve.wait_ge(*own.last)
                        dve.tensor_reduce(nmx[:, u % 3:u % 3 + 1], dst[:, 0:n], AX.X, ALU.max, negate=True).then_inc(*own.tell(att_s_out, att_s_out.at(l, u + 1)))
                    u = step + 1
                    if 0 <= u < NAT:
                        dve.wait_ge(att_exp.sem, att_exp.at(l, u + 1))
                        if u >= 3:
                            dve.wait_ge(att_p.sem, att_p.at(l, u - 2))
                        dve.reciprocal(rinv[:, u % 3:u % 3 + 1], sums[:, u % 3:u % 3 + 1]).then_inc(*own.tell(att_rinv, att_rinv.at(l, u + 1)))
                    u = step - 1
                    if 0 <= u:
                        b, hd, i = ATT_UNITS[u]
                        at, q = (HD * (hd % 2), NAQ + hd // 2) if b == "na" else (HD * (hd // 2), SQ + hd % 2)
                        dve.wait_ge(att_o_full.sem, att_o_full.at(l, u + 1))
                        dve.tensor_copy(fm[at:at + HD, q, i * P:(i + 1) * P], ps[at:at + HD, 6 + u % 2, 0:P]).then_inc(*own.tell(att_o_out, att_o_out.at(l, u + 1)))

            def first_of(dst, eq, tk):
                dve.wait_ge(*own.last)
                dve.tensor_copy(dst[:, :, 0:1], eq[:, :, 0:1]).then_inc(*own.step())
                dve.tensor_copy(tk[:, :, 0:1], eq[:, :, 0:1]).then_inc(*own.step())
                for j in range(1, 4):
                    dve.wait_ge(*own.last)
                    dve.tensor_tensor(dst[:, :, j:j + 1], eq[:, :, j:j + 1], tk[:, :, j - 1:j], ALU.is_gt).then_inc(*own.step())
                    if j < 3:
                        dve.tensor_tensor(tk[:, :, j:j + 1], eq[:, :, j:j + 1], tk[:, :, j - 1:j], ALU.max).then_inc(*own.step())

            def router(l):
                four = [P, TILES, 4]

                def row(k):
                    return rt[:, k, :, :]

                def col(k):
                    return rt[:, 11, :, k:k + 1]
                eq, tk, og, esel, oh1, oh2, es2, ce, tmp = (row(k) for k in range(9))
                gm, gs, m1, m2 = (col(k) for k in range(4))
                gex, dlt = rt[:, 12, :, :], rt[:, 13, :, 0:1]
                w1, w2 = rt[:, 10, :, 0:1], rt[:, 10, :, 1:2]
                dve.wait_ge(router_full.sem, router_full.at(l, 1))
                dve.tensor_tensor(lt[:, :, :], ps[:, 6, 0:100].rearrange("p (i e) -> p i e", e=20), pb("rb").unsqueeze(1).to_broadcast([P, TILES, 20]), ALU.add).then_inc(*own.step())
                dve.wait_ge(*own.last)
                g4 = lt[:, :, 0:4]
                dve.tensor_reduce(gm, g4, AX.X, ALU.max).then_inc(*own.step())
                dve.wait_ge(*own.last)
                dve.tensor_tensor(eq, g4, gm.to_broadcast(four), ALU.is_equal).then_inc(*own.step())
                dve.tensor_tensor(gex, g4, gm.to_broadcast(four), ALU.subtract).then_inc(*own.tell(r_in, r_in.at(l, 1)))
                first_of(og, eq, tk)
                dve.wait_ge(*own.last)
                dve.tensor_copy(og, og).then_inc(*own.tell(group_ready, group_ready.at(l, 1)))
                sort(l)
                for g in range(GROUPS):
                    e4 = lt[:, :, 4 + 4 * g:8 + 4 * g]
                    if g == 0:
                        dve.tensor_tensor(esel, e4, og[:, :, 0:1].to_broadcast(four), ALU.mult).then_inc(*own.step())
                        continue
                    dve.tensor_tensor(tmp, e4, og[:, :, g:g + 1].to_broadcast(four), ALU.mult).then_inc(*own.step())
                    dve.wait_ge(*own.last)
                    dve.tensor_tensor(esel, esel, tmp, ALU.add).then_inc(*own.step())
                    dve.wait_ge(*own.last)
                dve.tensor_reduce(m1, esel, AX.X, ALU.max).then_inc(*own.step())
                dve.wait_ge(*own.last)
                dve.tensor_tensor(eq, esel, m1.to_broadcast(four), ALU.is_equal).then_inc(*own.step())
                first_of(oh1, eq, tk)
                dve.wait_ge(*own.last)
                dve.scalar_tensor_tensor(out=es2, in0=oh1, scalar=NEG, in1=esel, op0=ALU.mult, op1=ALU.add).then_inc(*own.step())
                dve.wait_ge(*own.last)
                dve.tensor_reduce(m2, es2, AX.X, ALU.max).then_inc(*own.step())
                dve.wait_ge(*own.last)
                dve.tensor_tensor(dlt, m2, m1, ALU.subtract).then_inc(*own.tell(r_in, r_in.at(l, 2)))
                dve.tensor_tensor(eq, es2, m2.to_broadcast(four), ALU.is_equal).then_inc(*own.step())
                first_of(oh2, eq, tk)
                dve.wait_ge(r_exp.sem, r_exp.at(l, 2))
                dve.tensor_reduce(gs, gex, AX.X, ALU.add).then_inc(*own.step())
                dve.tensor_scalar(w1, dlt, 1.0, None, ALU.add).then_inc(*own.step())
                dve.wait_ge(*own.last)
                dve.tensor_tensor(w1, w1, gs, ALU.mult).then_inc(*own.step())
                dve.wait_ge(*own.last)
                dve.reciprocal(w1, w1).then_inc(*own.step())
                dve.wait_ge(*own.last)
                dve.tensor_tensor(w2, w1, dlt, ALU.mult).then_inc(*own.step())
                dve.tensor_tensor(oh1, oh1, w1.to_broadcast(four), ALU.mult).then_inc(*own.step())
                dve.wait_ge(*own.last)
                dve.tensor_tensor(oh2, oh2, w2.to_broadcast(four), ALU.mult).then_inc(*own.step())
                dve.wait_ge(*own.last)
                dve.tensor_tensor(ce, oh1, oh2, ALU.add).then_inc(*own.tell(weight_ready, weight_ready.at(l, 1)))

            dve.wait_ge(loaded, 16 * n_loads)
            first(dve.tensor_copy(msk[:, :, :, :].rearrange("p d l t -> p (d l) t"), mraw))
            with dve.Fori(0, DEPTH) as l:
                own.layer(l)
                dve.tensor_copy(lpc[:, :], lpb[:, l, :]).then_inc(*own.step())
                dve.tensor_scalar(omlb[:, :], lbs[:, l, :], -1.0, 1.0, ALU.mult, ALU.add).then_inc(*own.step())
                dve.memset(st[:, :, 0, :, :], 0.0).then_inc(*own.tell(small_ready, small_ready.at(l, 1)))
                dve.wait_ge(*own.last)
                for k, j in enumerate(PARTS["ada"]):
                    run_job(l, START["ada"] + k, j)
                norm_x(l, 0)
                dve.wait_ge(h_ready.sem, h_ready.at(l, KT))
                for k, j in enumerate(PARTS["hgrn_in"]):
                    run_job(l, START["hgrn_in"] + k, j)
                    if j.kind == "ada" and j.arg in (9, 10):
                        forget(l, j.arg - 9)
                    if j.kind == "fm" and j.arg[:2] == ("hq", HQ):
                        for d in range(2):
                            dve.wait_ge(ln_out.sem, ln_out.at(l, d + 1))
                            v = lf[:, :, d * BW:(d + 1) * BW]
                            dve.tensor_tensor(v, v, lnb[:, d, :, :], ALU.add).then_inc(*own.tell(f_ready, f_ready.at(l, d + 1)))
                dve.wait_ge(params_loaded.sem, params_loaded.at(l, 32))
                v = nab.rearrange("p e (r c) -> p (e r) c", c=HD)
                dve.tensor_tensor(v, v, c("nam").unsqueeze(1).to_broadcast([P, HEADS * 14, HD]), ALU.add).then_inc(*own.step())
                hgrn(l)
                hgrn_norm(l)
                adas = [j for j in PARTS["mix_in"] if j.kind == "ada"]
                sum_ada(l, adas.pop(0))
                for k, j in enumerate(PARTS["mix_in"]):
                    run_job(l, START["mix_in"] + k, j)
                    if j.kind == "ada" and adas:
                        sum_ada(l, adas.pop(0))
                    if j.kind == "ada" and j.arg == 16:
                        mlp_norm(l)
                attention(l)
                dve.wait_ge(kv_out.sem, kv_out.at(l, 5 * 16))
                adas = [j for j in PARTS["out"] if j.kind == "ada"]
                for part in ("merge", "out"):
                    for k, j in enumerate(PARTS[part]):
                        run_job(l, START[part] + k, j)
                        if j.kind == "out" and j.arg % 2 == 0:
                            sum_ada(l, adas.pop(0))
                norm_x(l, 1)
                router(l)
                run_job(l, START["moe"] - 1, PARTS["sort"][-1])
                unsorting(l)
                dve.wait_ge(*own.last)
                alone(dve)
                with dve.Fori(0, NBLK - 1) as g:
                    own.group(g)
                    block(l, g, PARTS["moe"])
                    own.end_group()
                block(l, NBLK - 1, PARTS["moe_last"])
                for k, j in enumerate(PARTS["back"]):
                    run_job(l, START["back"] + k, j)
                own.end_layer()
            own.layer(DEPTH)
            norm_x(DEPTH, 0)

        @block.gpsimd
        def _(pool):
            with pool.Fori(0, DEPTH) as l:
                for u, (d, stream, i) in enumerate(HGRN_UNITS):
                    v = u % 2
                    pool.wait_ge(kT_ready.sem, kT_ready.at(l, u + 1))
                    for a in range(2):
                        pool.wait_ge(ex_ready.sem, ex_ready.at(l, 2 * u + a + 1))
                        pool.tensor_tensor(ke[v][:, a, :, :], ex[v][:, a, 0:LEVELS, :],
                                           kT[v][:, a, :].unsqueeze(1).to_broadcast([P, LEVELS, P]), ALU.mult)\
                            .then_inc(ke_ready.sem, 1)
                    pool.wait_ge(es_ready.sem, es_ready.at(l, u + 1))
                    if u >= 2:
                        pool.wait_ge(o_full.sem, o_full.at(l, u - 1))
                    pool.tensor_tensor(kd[v], kk[:, i, d * BW:(d + 1) * BW], es[v], ALU.mult).then_inc(kd_ready.sem, 1)
                for u, (b, hd, i) in enumerate(ATT_UNITS):
                    n = n_keys(b, i)
                    pool.wait_ge(att_rinv.sem, att_rinv.at(l, u + 1))
                    alone(pool)
                    pool.tensor_scalar(sbs[:, u % 3, 0:n], sbs[:, u % 3, 0:n], rinv[:, u % 3:u % 3 + 1], None,
                                       ALU.mult).then_inc(att_p.sem, 1)


def constants():
    r = np.arange(P)
    cst = {}
    cst["ident"] = np.eye(P)
    cst["ones"] = np.ones((P, P))
    cst["block"] = (r[:, None] // HD == r[None, :] // HD) * 1.0
    perm = np.zeros((P, P))
    for m in range(P):
        if m % 32 < 16:
            perm[m + 16, m] = -1.0
        else:
            perm[m - 16, m] = 1.0
    cst["perm"] = perm
    decay = np.zeros((P, 2, 8, P))
    mask = np.zeros((P, 2, LEVELS, HD), np.float32)
    rr, t = r[:, None], r[None, :]
    for lev in range(LEVELS):
        half = HD >> lev
        mid = t // (2 * half) * (2 * half) + half
        second = t >= mid
        decay[:, 0, lev] = np.where(second, (rr >= mid) & (rr <= t), (rr > t) & (rr < mid))
        decay[:, 1, lev] = np.where(second, (rr >= mid) & (rr < t), (rr >= t) & (rr < mid))
        block = r // (2 * half)
        in_second = r % (2 * half) >= half
        for d in range(2):
            queries = np.nonzero(in_second == (d == 0))[0]
            mask[:, d, lev] = (block[:, None] == block[queries][None, :]) & (in_second[:, None] == (d == 1))
    decay[:, 0, 7] = rr <= t
    decay[:, 1, 7] = rr >= t
    cst["decay"] = decay.reshape(P, -1)
    tail = np.zeros((P, 2, P))
    tail[:, 0] = rr > t
    tail[:, 1] = rr < t
    cst["tail"] = tail.reshape(P, -1)
    f = np.float32
    inv = (f(1.0) / (f(10000.0) ** (np.arange(0, 32, 2, dtype=f) / f(32)))).astype(f)
    tok = np.arange(LAT)
    ang = np.zeros((HD, LAT), f)
    for m in range(HD):
        pos = (tok // 64 if m < 32 else tok % 64).astype(f)
        ang[m] = pos * inv[m % 16]
    cst["cos"] = np.tile(np.cos(ang), (2, 1))
    cst["sin"] = np.tile(np.sin(ang), (2, 1))
    swm = np.zeros((P, 3, P))
    swm[:, 0] = np.where(t >= rr, 0, NEG)
    swm[:, 2] = np.where(t <= rr, 0, NEG)
    cst["swm"] = swm.reshape(P, -1)
    col = r % 64
    start = np.clip(col - 8, 0, 48)[:, None]
    c2 = np.arange(64)[None, :]
    cst["nam"] = np.where((c2 >= start) & (c2 < start + 16), 0, NEG)
    cst["iota"] = np.broadcast_to(r[None, :], (P, P))
    cst["slotid"] = r[:, None] + P * np.arange(NBLK)[None, :]
    cst["blockid"] = np.broadcast_to(np.arange(NBLK)[None, :], (P, NBLK))
    flat = np.concatenate([cst[name].astype(f) for name in CST], axis=1)
    assert flat.shape[1] == N_CST
    return np.ascontiguousarray(flat), mask.reshape(P, 2 * LEVELS, HD)


def fmaj(a):
    return np.asarray(a).reshape(-1, P, a.shape[-1]).transpose(1, 0, 2)


def lay_out(inp):
    inp = {k: np.asarray(v) for k, v in inp.items()}
    f = np.float32
    cst, mask = constants()
    arrays = {"cst": cst, "msk": mask}
    arrays["xT"] = fmaj(np.concatenate([inp["x_sample"][0], inp["x_prompt"][0]], 0).T)
    arrays["cT"] = fmaj(np.stack([inp["c"][0], inp["c_ctx"]], 1))
    arrays["fg"] = inp["final_g"].reshape(KT, P).T
    arrays["lbr"] = np.broadcast_to(inp["hgrn_lb"].reshape(1, DEPTH, 2 * BW), (P, DEPTH, 2 * BW))
    sw = np.concatenate([np.arange(hh * HD, (hh + 1) * HD) for hh in (0, 2, 1, 3)])
    ws = np.empty((DEPTH * DRAM_PAIRS, P, 2, UNIT), f)
    lpa = np.empty((DEPTH, P, N_LPA), f)
    lpb = np.empty((P, DEPTH, N_LPB), f)
    for l in range(DEPTH):
        w_in = inp["w_in"][l].copy()
        w_in[:, COL["sq"]:COL["sq"] + BW] = w_in[:, COL["sq"] + sw]
        w_branch = inp["w_branch"][l].copy()
        w_branch[3] = w_branch[3][sw]

        def cols(w, c0, n=P):
            return w[:, c0:c0 + n].reshape(-1, P, n).transpose(1, 0, 2)

        def put(u, spec, g=0):
            dst = ws[l * DRAM_PAIRS + u // 2, :, u % 2]
            kind = spec[0]
            if kind == "ada":
                v = cols(inp["w_ada"][l], spec[1] * P)
            elif kind == "in":
                v = cols(w_in, spec[1])
            elif kind == "tm":
                v = cols(w_in, spec[1], 256).reshape(P, 2, UNIT)[:, spec[2]]
            elif kind == "branch":
                v = cols(w_branch.reshape(NB * BW, D), spec[1] * P)
            elif kind == "out":
                v = cols(inp["w_out"][l], spec[1] * P)
            elif kind in ("moe_gate", "moe_up"):
                w = inp["moe_w_gate" if kind == "moe_gate" else "moe_w_up"][l, g * EPG + spec[1]]
                v = cols(w, spec[2] * P)
            elif kind == "moe_down":
                v = inp["moe_w_down"][l, g * EPG + spec[1], spec[2] * P:(spec[2] + 1) * P]
            dst[...] = v.reshape(P, UNIT)

        for u, spec in enumerate(UNITS0):
            put(u, spec)
        for g in range(GROUPS):
            for u, spec in enumerate(UNITS_G):
                put(len(UNITS0) + g * len(UNITS_G) + u, spec, g)

        parts = {}
        q = np.arange(P)
        e = np.arange(14)
        dr = e[None, :] + 1 - (q[:, None] >= 64)
        dc = np.clip(np.arange(64)[None, :] - (q[:, None] % 64), -15, 15) + 15
        rpb = inp["na_rpb"][l]
        parts["nab"] = rpb[:, dr[:, :, None], dc[:, None, :]].transpose(1, 0, 2, 3)
        parts["nk"] = fmaj(inp["cache_na_k"][0, l].reshape(P, BW).T)
        parts["nv"] = inp["cache_na_v"][0, l].reshape(P, BW)
        parts["sk"] = inp["cache_swa_k"][0, l].reshape(P, P).T
        parts["sv"] = inp["cache_swa_v"][0, l].reshape(P, P)
        parts["ws"] = inp["smlp_ws"][l].transpose(2, 0, 1)
        parts["smb"] = np.repeat(inp["smlp_b"][l].reshape(2, 2, 1, P), HD, 2).reshape(2, P, P).transpose(1, 0, 2)
        parts["sink"] = np.broadcast_to(inp["swa_sink"][l][None], (P, HEADS))
        lpa[l] = np.concatenate([parts[k].reshape(P, -1) for k in LPA], 1)
        parts["b_ada"] = inp["b_ada"][l].reshape(48, P).T
        parts["n1"] = inp["norm1_g"][l].reshape(KT, P).T
        parts["n2"] = inp["norm2_g"][l].reshape(KT, P).T
        parts["on"] = inp["hgrn_onorm_g"][l].reshape(2, P).T
        parts["wr"] = fmaj(np.concatenate([inp["router_g_w"][l], inp["router_e_w"][l]], 1))
        parts["rb"] = np.broadcast_to(np.concatenate([inp["router_g_b"][l], inp["router_e_b"][l]])[None], (P, 20))
        lpb[:, l] = np.concatenate([parts[k].reshape(P, -1) for k in LPB], 1)
    arrays["ws"] = ws.reshape(DEPTH * DRAM_PAIRS, P, 2 * UNIT)
    arrays["lpa"] = lpa
    arrays["lpb"] = lpb
    s = inp["state_hgrn"][0].reshape(DEPTH, 2, 2, 2, HD, HD)
    arrays["st_in"] = s.transpose(0, 3, 4, 1, 2, 5).reshape(DEPTH, P, 2, 2, HD)
    return {k: np.ascontiguousarray(v) for k, v in arrays.items()}


OUTS = {
    "y": (P, KT, T), "nk_out": (DEPTH, P, 2, P), "nv_out": (DEPTH, P, BW), "sk_out": (DEPTH, P, P),
    "sv_out": (DEPTH, P, P), "st_out": (DEPTH, P, 2, 2, HD),
}


def make(nc, arrays):
    A = {k: nc.dram_tensor(k, v.shape, mybir.dt.from_np(v.dtype), kind="ExternalInput").ap() for k, v in arrays.items()}
    for k, shape in OUTS.items():
        A[k] = nc.dram_tensor(k, shape, F32, kind="ExternalOutput").ap()
    build(nc, A)
    return nc


def unpack(r):
    y = r["y"].transpose(2, 1, 0).reshape(T, D)
    nk = r["nk_out"].transpose(0, 3, 2, 1).reshape(1, DEPTH, CTX, HEADS, HD)
    nv = r["nv_out"].reshape(1, DEPTH, CTX, HEADS, HD)
    sk = r["sk_out"].transpose(0, 2, 1).reshape(1, DEPTH, CTX, 2, HD)
    sv = r["sv_out"].reshape(1, DEPTH, CTX, 2, HD)
    s = r["st_out"].reshape(DEPTH, 2, HD, 2, 2, HD).transpose(0, 3, 4, 1, 2, 5).reshape(1, DEPTH, 2, HEADS, HD, HD)
    out = (y[LAT:][None], y[:LAT][None], nk, nv, sk, sv, s)
    return tuple(np.ascontiguousarray(v) for v in out)


def kernel(**inputs):
    import concourse.bacc as bacc
    from concourse.bass_utils import run_bass_kernel_spmd

    arrays = lay_out(inputs)
    nc = bacc.Bacc("TRN2", target_bir_lowering=False, num_devices=1)
    make(nc, arrays)
    r = run_bass_kernel_spmd(nc, [arrays], core_ids=[0])
    return unpack(r.results[0])
```
